# Optimizing a Trainium2 kernel written in Bass

```python
import jax, jax.numpy as jnp
from jax import lax
import numpy as np

D_MODEL = 1024
BATCH = 1
SEQ = 512
DEPTH = 2
DEC_BATCH = 1
DEC_SEQ = 64
PAST_LEN = 512

CHUNK = 64
Q_BLOCK = 128
EPS = 1e-6
F32 = jnp.float32

RW_HEADS = 8
RW_HEAD_DIM = 64
RW_WIDTH = RW_HEADS * RW_HEAD_DIM
RW_DECAY_LORA = 64
RW_ICLR_LORA = 64
RW_GATE_LORA = 128
RW_SPLITS = (RW_WIDTH, RW_WIDTH, RW_WIDTH, RW_DECAY_LORA, RW_ICLR_LORA, RW_GATE_LORA)
RW_COLS = sum(RW_SPLITS)
RW_GN_EPS = 64e-5

SA_HEADS = 8
SA_KV_HEADS = 2
SA_HEAD_DIM = 64
SA_WIDTH = SA_HEADS * SA_HEAD_DIM
IDX_HEADS = 4
IDX_DIM = 64
TOPK_MAX = 256
ROPE_THETA = 500000.0
ROPE_DIM = SA_HEAD_DIM // 4
INDEX_SCALE = (IDX_DIM ** -0.5) * (IDX_HEADS ** -0.5)
SA_SPLITS = (SA_WIDTH, SA_KV_HEADS * SA_HEAD_DIM, SA_KV_HEADS * SA_HEAD_DIM, IDX_HEADS * IDX_DIM, IDX_DIM, IDX_HEADS)
SA_COLS = sum(SA_SPLITS)

RET_HEADS = 4
RET_HEAD_DIM = 128
RET_WIDTH = RET_HEADS * RET_HEAD_DIM
RET_ROPE_BASE = 10000.0
RET_COLS = 4 * RET_WIDTH

N_BRANCH = 3
GATE_COLS = N_BRANCH * D_MODEL
IN_COLS = RW_COLS + SA_COLS + RET_COLS + GATE_COLS
D_FF = 4 * D_MODEL

kernel_name = 'hybrid_rwkv7_dsa_retention_stream_step'

def rmsnorm(x, g):
    xf = x.astype(F32)
    y = xf * lax.rsqrt(jnp.mean(xf * xf, axis=-1, keepdims=True) + EPS)
    return (y * g.astype(F32)).astype(x.dtype)

def split_cols(t, widths):
    return jnp.split(t, [int(c) for c in np.cumsum(widths)[:-1]], axis=-1)

def apply_rotary(x, pos, freqs):
    half = freqs.shape[0]
    rot = 2 * half
    xf = x.astype(F32)
    ang = pos.astype(F32)[:, None] * freqs[None, :]
    cos = jnp.cos(ang)[:, None, :]
    sin = jnp.sin(ang)[:, None, :]
    x1, x2 = xf[..., :half], xf[..., half:rot]
    out = jnp.concatenate([x1 * cos - x2 * sin, x2 * cos + x1 * sin, xf[..., rot:]], axis=-1)
    return out.astype(x.dtype)

def partial_rope_freqs():
    return 1.0 / (ROPE_THETA ** (jnp.arange(0, ROPE_DIM, 2, dtype=F32) / ROPE_DIM))

def retention_freqs():
    return 1.0 / (RET_ROPE_BASE ** jnp.linspace(0.0, 1.0, RET_HEAD_DIM // 2, dtype=F32))

def rwkv_scan(r, decay, k, v, kk, a, S0):
    def step(S, inp):
        r_t, w_t, k_t, v_t, kk_t, a_t = inp
        removed = jnp.einsum('bhvk,bhk->bhv', S, kk_t)
        S = (S * w_t[:, :, None, :]
             - removed[..., None] * (kk_t * a_t)[:, :, None, :]
             + v_t[..., None] * k_t[:, :, None, :])
        return S, jnp.einsum('bhvk,bhk->bhv', S, r_t)
    xs = tuple(jnp.moveaxis(t, 1, 0) for t in (r, decay, k, v, kk, a))
    S, y = lax.scan(step, S0, xs)
    return jnp.moveaxis(y, 0, 1), S

def rwkv_mixer(P, shift_prev, S0, lp):
    B, L, _ = P.shape
    prev = jnp.concatenate([shift_prev[:, None, :].astype(P.dtype), P[:, :-1]], axis=1)
    X = P + (prev - P) * lp['rwkv_mu']
    r, k, v, xw, xa, xg = split_cols(X.astype(F32), RW_SPLITS)
    w = -jax.nn.softplus(-(lp['rwkv_w0'].astype(F32) + jnp.tanh(xw) @ lp['rwkv_w2'].astype(F32))) - 0.5
    decay = jnp.exp(-jnp.exp(w))
    a = jax.nn.sigmoid(lp['rwkv_a0'].astype(F32) + xa @ lp['rwkv_a2'].astype(F32))
    g = jax.nn.sigmoid(xg) @ lp['rwkv_g2'].astype(F32)
    hv = lambda t: t.reshape(B, L, RW_HEADS, RW_HEAD_DIM)
    hp = lambda t: t.astype(F32).reshape(RW_HEADS, RW_HEAD_DIM)
    r, k, v, decay, a = hv(r), hv(k), hv(v), hv(decay), hv(a)
    kk = k * hp(lp['rwkv_k_k'])
    kk = kk / jnp.maximum(jnp.sqrt(jnp.sum(kk * kk, axis=-1, keepdims=True)), 1e-12)
    k = k * (1.0 + (a - 1.0) * hp(lp['rwkv_k_a']))
    y, S = rwkv_scan(r, decay, k, v, kk, a, S0.astype(F32))
    mean = jnp.mean(y, axis=-1, keepdims=True)
    var = jnp.mean(jnp.square(y - mean), axis=-1, keepdims=True)
    y = (y - mean) * lax.rsqrt(var + RW_GN_EPS) * hp(lp['rwkv_lnx_g'])
    y = y + jnp.sum(r * k * lp['rwkv_r_k'].astype(F32), axis=-1, keepdims=True) * v
    y = y.reshape(B, L, RW_WIDTH) * g
    return y.astype(P.dtype), S, P[:, -1]

def dsa_block(q, qi, wi, k_all, v_all, ki_all, limit, topk):
    B, Qb = q.shape[:2]
    Lk = k_all.shape[1]
    dots = jnp.einsum('bqhd,bsd->bqhs', qi.astype(F32), ki_all.astype(F32))
    score = jnp.einsum('bqhs,bqh->bqs', jax.nn.relu(dots), wi.astype(F32)) * INDEX_SCALE
    admissible = jnp.arange(Lk)[None, :] < limit[:, None]
    score = jnp.where(admissible[None], score, -jnp.inf)
    _, idx = lax.top_k(score, topk)
    valid = idx < limit[None, :, None]
    k_sel = jax.vmap(lambda t, i: t[i])(k_all, idx)
    v_sel = jax.vmap(lambda t, i: t[i])(v_all, idx)
    qg = q.astype(F32).reshape(B, Qb, SA_KV_HEADS, SA_HEADS // SA_KV_HEADS, SA_HEAD_DIM)
    logits = jnp.einsum('bqcgd,bqncd->bqcgn', qg, k_sel.astype(F32)) * (SA_HEAD_DIM ** -0.5)
    logits = jnp.where(valid[:, :, None, None, :], logits, -jnp.inf)
    p = jax.nn.softmax(logits, axis=-1)
    o = jnp.einsum('bqcgn,bqncd->bqcgd', p, v_sel.astype(F32))
    return o.reshape(B, Qb, SA_WIDTH)

def dsa_mixer(P, pos, k_past, v_past, ik_past):
    B, L, _ = P.shape
    q, k, v, qi, ki, wi = split_cols(P, SA_SPLITS)
    freqs = partial_rope_freqs()
    q = apply_rotary(q.reshape(B, L, SA_HEADS, SA_HEAD_DIM), pos, freqs)
    k = apply_rotary(k.reshape(B, L, SA_KV_HEADS, SA_HEAD_DIM), pos, freqs)
    v = v.reshape(B, L, SA_KV_HEADS, SA_HEAD_DIM)
    qi = apply_rotary(qi.reshape(B, L, IDX_HEADS, IDX_DIM), pos, freqs)
    ki = apply_rotary(ki.reshape(B, L, 1, IDX_DIM), pos, freqs)[:, :, 0]
    k_all = jnp.concatenate([k_past.astype(k.dtype), k], axis=1)
    v_all = jnp.concatenate([v_past.astype(v.dtype), v], axis=1)
    ki_all = jnp.concatenate([ik_past.astype(ki.dtype), ki], axis=1)
    Lk = k_all.shape[1]
    topk = min(TOPK_MAX, Lk // 4)
    limit = jnp.minimum((pos // CHUNK + 1) * CHUNK, Lk)
    qb = min(Q_BLOCK, L)
    nb = L // qb
    blocks = lambda t: jnp.moveaxis(t.reshape((B, nb, qb) + t.shape[2:]), 1, 0)

    def attend(args):
        q_b, qi_b, wi_b, lim_b = args
        return dsa_block(q_b, qi_b, wi_b, k_all, v_all, ki_all, lim_b, topk)

    o = lax.map(attend, (blocks(q), blocks(qi), blocks(wi), limit.reshape(nb, qb)))
    y = jnp.moveaxis(o, 0, 1).reshape(B, L, SA_WIDTH)
    return y.astype(P.dtype), k, v, ki

def retention_chunk(q, k, v, S, log_gamma):
    c = q.shape[1]
    idx = jnp.arange(c, dtype=F32)
    dist = jnp.abs(idx[:, None] - idx[None, :])
    dmask = jnp.exp(dist[None] * log_gamma[:, None, None])
    scores = jnp.einsum('bqhd,bmhd->bhqm', q, k) * dmask[None]
    intra = jnp.einsum('bhqm,bmhe->bqhe', scores, v)
    q_decay = jnp.exp((idx[:, None] + 1.0) * log_gamma[None, :])
    cross = jnp.einsum('bqhd,bhde->bqhe', q, S) * q_decay[None, :, :, None]
    k_decay = jnp.exp((c - 1.0 - idx)[:, None] * log_gamma[None, :])
    S_new = (S * jnp.exp(c * log_gamma)[None, :, None, None]
             + jnp.einsum('bmhd,bmhe->bhde', k * k_decay[None, :, :, None], v))
    return intra + cross, S_new

def retention_mixer(P, pos, S0):
    B, L, _ = P.shape
    q, k, v, g = split_cols(P, (RET_WIDTH,) * 4)
    hv = lambda t: t.astype(F32).reshape(B, L, RET_HEADS, RET_HEAD_DIM)
    freqs = retention_freqs()
    q = apply_rotary(hv(q), pos, freqs)
    k = apply_rotary(hv(k), pos, freqs) * (RET_HEAD_DIM ** -0.5)
    v = hv(v)
    log_gamma = jnp.log1p(-jnp.exp2(-5.0 - jnp.arange(RET_HEADS, dtype=F32)))
    c = min(CHUNK, L)
    nc = L // c
    chunks = lambda t: jnp.moveaxis(t.reshape(B, nc, c, RET_HEADS, t.shape[-1]), 1, 0)

    def step(S, inp):
        qc, kc, vc = inp
        o, S = retention_chunk(qc, kc, vc, S, log_gamma)
        return S, o

    S, o = lax.scan(step, S0.astype(F32), (chunks(q), chunks(k), chunks(v)))
    o = jnp.moveaxis(o, 0, 1).reshape(B, L, RET_HEADS, RET_HEAD_DIM)
    o = o * lax.rsqrt(jnp.mean(o * o, axis=-1, keepdims=True) + EPS)
    y = jax.nn.silu(g.astype(F32)) * o.reshape(B, L, RET_WIDTH)
    return y.astype(P.dtype), S

def trunk_layer(x, past, lp):
    k_past, v_past, ik_past, s_rw, shift_rw, s_ret = past
    B, L, _ = x.shape
    pos = k_past.shape[1] + jnp.arange(L, dtype=jnp.int32)
    h = rmsnorm(x, lp['norm1_g'])
    P = h @ lp['w_in']
    P_rw, P_sa, P_ret, P_gate = split_cols(P, (RW_COLS, SA_COLS, RET_COLS, GATE_COLS))
    y_rw, s_rw_new, shift_new = rwkv_mixer(P_rw, shift_rw, s_rw, lp)
    y_sa, k_new, v_new, ik_new = dsa_mixer(P_sa, pos, k_past, v_past, ik_past)
    y_ret, s_ret_new = retention_mixer(P_ret, pos, s_ret)
    gates = jax.nn.sigmoid(P_gate.astype(F32)).astype(x.dtype).reshape(B, L, N_BRANCH, D_MODEL)
    merged = (gates[:, :, 0] * (y_rw @ lp['w_br_rwkv'])
              + gates[:, :, 1] * (y_sa @ lp['w_br_dsa'])
              + gates[:, :, 2] * (y_ret @ lp['w_br_ret']))
    x = x + merged @ lp['w_o']
    h2 = rmsnorm(x, lp['norm2_g'])
    x = x + jnp.square(jax.nn.relu(h2 @ lp['w_up'])) @ lp['w_down']
    return x, (k_new, v_new, ik_new, s_rw_new, shift_new, s_ret_new)

def setup_inputs(seed: int = 0) -> dict:
    key = jax.random.key(seed)
    ks = iter(jax.random.split(key, 32))
    nrm = lambda shape, scale: jax.random.normal(next(ks), shape, F32) * scale
    D = D_MODEL
    return {
        'x_prompt': nrm((BATCH, SEQ, D), 1.0),
        'x_sample': nrm((DEC_BATCH, DEC_SEQ, D), 1.0),
        'cache_dsa_k': nrm((DEPTH, DEC_BATCH, PAST_LEN, SA_KV_HEADS, SA_HEAD_DIM), 1.0),
        'cache_dsa_v': nrm((DEPTH, DEC_BATCH, PAST_LEN, SA_KV_HEADS, SA_HEAD_DIM), 1.0),
        'cache_dsa_ik': nrm((DEPTH, DEC_BATCH, PAST_LEN, IDX_DIM), 1.0),
        'state_rwkv': nrm((DEPTH, DEC_BATCH, RW_HEADS, RW_HEAD_DIM, RW_HEAD_DIM), 1.0),
        'state_rwkv_shift': nrm((DEPTH, DEC_BATCH, RW_COLS), 1.0),
        'state_ret': nrm((DEPTH, DEC_BATCH, RET_HEADS, RET_HEAD_DIM, RET_HEAD_DIM), 1.0),
        'norm1_g': 1.0 + nrm((DEPTH, D), 0.05),
        'w_in': nrm((DEPTH, D, IN_COLS), D ** -0.5),
        'rwkv_mu': jax.random.uniform(next(ks), (DEPTH, RW_COLS), F32),
        'rwkv_w0': nrm((DEPTH, RW_WIDTH), 0.5),
        'rwkv_w2': nrm((DEPTH, RW_DECAY_LORA, RW_WIDTH), 0.5 * RW_DECAY_LORA ** -0.5),
        'rwkv_a0': nrm((DEPTH, RW_WIDTH), 0.1),
        'rwkv_a2': nrm((DEPTH, RW_ICLR_LORA, RW_WIDTH), 0.5 * RW_ICLR_LORA ** -0.5),
        'rwkv_g2': nrm((DEPTH, RW_GATE_LORA, RW_WIDTH), RW_GATE_LORA ** -0.5),
        'rwkv_k_k': 0.85 + nrm((DEPTH, RW_WIDTH), 0.1),
        'rwkv_k_a': 1.0 + nrm((DEPTH, RW_WIDTH), 0.1),
        'rwkv_r_k': nrm((DEPTH, RW_HEADS, RW_HEAD_DIM), 0.1),
        'rwkv_lnx_g': 1.0 + nrm((DEPTH, RW_WIDTH), 0.05),
        'w_br_rwkv': nrm((DEPTH, RW_WIDTH, D), RW_WIDTH ** -0.5),
        'w_br_dsa': nrm((DEPTH, SA_WIDTH, D), SA_WIDTH ** -0.5),
        'w_br_ret': nrm((DEPTH, RET_WIDTH, D), RET_WIDTH ** -0.5),
        'w_o': nrm((DEPTH, D, D), D ** -0.5),
        'norm2_g': 1.0 + nrm((DEPTH, D), 0.05),
        'w_up': nrm((DEPTH, D, D_FF), D ** -0.5),
        'w_down': nrm((DEPTH, D_FF, D), D_FF ** -0.5),
        'final_norm_g': 1.0 + nrm((D,), 0.05),
    }

def reference(x_prompt, x_sample, cache_dsa_k, cache_dsa_v, cache_dsa_ik, state_rwkv,
              state_rwkv_shift, state_ret, norm1_g, w_in, rwkv_mu, rwkv_w0, rwkv_w2,
              rwkv_a0, rwkv_a2, rwkv_g2, rwkv_k_k, rwkv_k_a, rwkv_r_k, rwkv_lnx_g,
              w_br_rwkv, w_br_dsa, w_br_ret, w_o, norm2_g, w_up, w_down, final_norm_g):
    params = {
        'norm1_g': norm1_g, 'w_in': w_in, 'rwkv_mu': rwkv_mu, 'rwkv_w0': rwkv_w0,
        'rwkv_w2': rwkv_w2, 'rwkv_a0': rwkv_a0, 'rwkv_a2': rwkv_a2, 'rwkv_g2': rwkv_g2,
        'rwkv_k_k': rwkv_k_k, 'rwkv_k_a': rwkv_k_a, 'rwkv_r_k': rwkv_r_k,
        'rwkv_lnx_g': rwkv_lnx_g, 'w_br_rwkv': w_br_rwkv, 'w_br_dsa': w_br_dsa,
        'w_br_ret': w_br_ret, 'w_o': w_o, 'norm2_g': norm2_g, 'w_up': w_up, 'w_down': w_down,
    }
    Bp = x_prompt.shape[0]
    dt = x_prompt.dtype
    xp, xs = x_prompt, x_sample
    p_states = [[] for _ in range(6)]
    s_states = [[] for _ in range(6)]
    for i in range(DEPTH):
        lp = {name: arr[i] for name, arr in params.items()}
        past_p = (jnp.zeros((Bp, 0, SA_KV_HEADS, SA_HEAD_DIM), dt),
                  jnp.zeros((Bp, 0, SA_KV_HEADS, SA_HEAD_DIM), dt),
                  jnp.zeros((Bp, 0, IDX_DIM), dt),
                  jnp.zeros((Bp, RW_HEADS, RW_HEAD_DIM, RW_HEAD_DIM), F32),
                  jnp.zeros((Bp, RW_COLS), dt),
                  jnp.zeros((Bp, RET_HEADS, RET_HEAD_DIM, RET_HEAD_DIM), F32))
        past_s = (cache_dsa_k[i], cache_dsa_v[i], cache_dsa_ik[i],
                  state_rwkv[i], state_rwkv_shift[i], state_ret[i])
        xp, new_p = trunk_layer(xp, past_p, lp)
        xs, new_s = trunk_layer(xs, past_s, lp)
        for j in range(6):
            p_states[j].append(new_p[j])
            s_states[j].append(new_s[j])
    y_prompt = rmsnorm(xp, final_norm_g)
    y_sample = rmsnorm(xs, final_norm_g)
    p_k, p_v, p_ik, p_rwkv, p_shift, p_ret = [jnp.stack(t, axis=0) for t in p_states]
    s_k, s_v, s_ik, s_rwkv, s_shift, s_ret = [jnp.stack(t, axis=0) for t in s_states]
    return (y_prompt, y_sample, p_k, p_v, p_ik, p_rwkv, p_shift, p_ret,
            s_k, s_v, s_ik, s_rwkv, s_shift, s_ret)


_drawn_inputs = setup_inputs


def setup_inputs(seed=0):
    import zlib

    import numpy as np

    out = dict(_drawn_inputs(seed))
    spreads = {}
    factors = {'rwkv_lnx_g': 2.915}
    for name, (base, spread) in spreads.items():
        noise = np.random.default_rng([zlib.crc32(name.encode()), seed]).standard_normal(out[name].shape)
        drawn = base * np.exp(spread * noise) if base else spread * noise
        out[name] = __import__('jax').numpy.asarray(drawn.astype(out[name].dtype))
    for name, factor in factors.items():
        out[name] = (out[name] * factor).astype(out[name].dtype)
    return out
```

```python
from contextlib import ExitStack

import numpy as np

import concourse.bass as bass
from concourse import mybir

F32 = mybir.dt.float32
F32R = mybir.dt.float32r
ALU = mybir.AluOpType
ACT = mybir.ActivationFunctionType
AX_X = mybir.AxisListType.X
EXP_LN = "natural_log_exp_and_others"

P = 128
DEPTH = 2
D = 1024
KT = D // P
TP, TS = 512, 64
T = TP + TS
HALF = T // 2
TX = T + 1
SX = TP + 1
C = 64
NC = T // C
EPS = 1e-6
GN_EPS = 64e-5
DECAY = float(np.exp(-0.5))
SA_SCALE = 64 ** -0.5
IDX_SCALE = (64 ** -0.5) * (4 ** -0.5)
RET_SCALE = 128 ** -0.5
NEG = -1e30
FILL, MARK, EDGE = -3.0e38, -3.4e38, -3.2e38
TOPK_P = min(256, TP // 4)
TOPK_S = min(256, (TP + TS) // 4)
FF = 4

N_RET, N_SA, N_RW, N_GATE = 16, 9, 14, 24
T_RET = 0
T_SA = T_RET + N_RET
T_RW = T_SA + N_SA
T_GATE = T_RW + N_RW
T_SPARE = T_GATE + N_GATE
T_BR = T_SPARE + 1
T_WO = T_BR + 12
T_MLP = T_WO + KT
NT = T_MLP + FF * 2 * KT
RAW, SPLIT = 4, 2
assert NT % RAW == 0 and NT % SPLIT == 0

U_BR = T_BR
U_WO = U_BR + 24
U_MLP = U_WO + KT
NU = U_MLP + FF * 2 * KT
assert NU % 2 == 0

N_FILL = (N_RW + N_GATE) * KT
FILL_TOPK = (0, 18, 24, 28, 34)
FILL_HEAD = (3, 2)
assert sum(FILL_TOPK) + 5 * 8 * sum(FILL_HEAD) == N_FILL


def fill_range(b, h=None, part=0):
    first = sum(FILL_TOPK[:b]) + b * 8 * sum(FILL_HEAD)
    if h is None:
        return first, first + FILL_TOPK[b]
    first += FILL_TOPK[b] + h * sum(FILL_HEAD) + (FILL_HEAD[0] if part else 0)
    return first, first + FILL_HEAD[part]


def fill_done(b, h=None, part=0):
    first, end = fill_range(b, h, part)
    return range(first // KT, end // KT)


PARAMS = {}
for _name, _n in (("g1", 8), ("g2", 8), ("mu", 14), ("w0", 4), ("a0", 4), ("k_k", 4), ("k_a", 4),
                  ("r_k", 4), ("lnx", 4), ("shift", 14)):
    PARAMS[_name] = (sum(v[1] for v in PARAMS.values()), _n)
NPAR = sum(v[1] for v in PARAMS.values())

START = 1

M_STRICT, M_INCL, M_PAIR, M_PAIR_T, M_EYE, M_LEVEL = 0, 1, 2, 3, 4, 5
LEVELS = (2, 4, 8, 16, 32)
NMASK = M_LEVEL + len(LEVELS)


class Steps:

    def __init__(self, sem, names):
        self.sem, self.names = sem, list(names)

    def at(self, name, run=0):
        return run * len(self.names) + self.names.index(name) + 1


def free_before(u, layer):
    spare = 1 if (u % 2 == T_SPARE % 2 and u > T_SPARE) else 0
    per_layer = NU // 2 - (1 if u % 2 == T_SPARE % 2 else 0)
    return layer * per_layer + u // 2 - spare + START


def used_after(t, layer, half=0):
    return layer * (2 * NT) + 2 * t + (1 if half == 1 else 2)


def layer_of(t, l):
    return t[bass.ds(l, 1), :, :].rearrange("a p n -> p (a n)")


def build(nc, dr, outs):
    with ExitStack() as ctx:
        def sb(name, shape, dt=F32):
            return ctx.enter_context(nc.sbuf_tensor(name, shape, dt))

        def sem(name):
            return ctx.enter_context(nc.semaphore(name))

        x = sb("x", [P, KT, T])
        with nc.sbuf_tensor("region_c", [P, 2 * KT * T], F32) as region_c:
            pass
        act_hi = sb("act_hi", [P, KT, T], F32R)
        act_lo = sb("act_lo", [P, KT, T], F32R)
        w_raw = sb("w_raw", [P, RAW, 1024])
        w_hi = sb("w_hi", [P, SPLIT, 1024], F32R)
        w_lo = sb("w_lo", [P, SPLIT, 1024], F32R)
        ysa = sb("ysa", [P, 4, T])
        yret = sb("yret", [P, 4, T])
        cst = sb("cst", [P, 5 * P])
        ident, ones, blk, rot_sa, rot_ret = (cst[:, P * i:P * i + P] for i in range(5))
        masks = sb("masks", [P, NMASK, C])
        small = sb("small", [P, 16])
        par = sb("par", [P, NPAR])
        region_a = sb("region_a", [P, 4 * TX + 4])
        n_root = sb("n_root", [P, T])
        WORDS_B = 21184
        with nc.sbuf_tensor("region_b", [P, WORDS_B], F32) as region_b:
            pass
        in_hi = sb("in_hi", [P, 12, T], F32R)
        in_lo = sb("in_lo", [P, 12, T], F32R)
        ra = region_a

        class Carve:
            def __init__(self):
                self.at = 0

            def __call__(self, *shape):
                n = int(np.prod(shape))
                assert self.at + n <= WORDS_B, (self.at, n)
                v = region_b[:, self.at:self.at + n]
                self.at += n
                if len(shape) == 2:
                    v = v.rearrange("p (a b) -> p a b", b=shape[1])
                if len(shape) == 3:
                    v = v.rearrange("p (a b c) -> p a b c", b=shape[1], c=shape[2])
                return v

        n_sq = ra[:, 0:2 * T].rearrange("p (a b) -> p a b", b=T)
        n_t = ra[:, 2 * T:4 * T].rearrange("p (a b) -> p a b", b=T)
        n_rs = n_root[:, :]
        cr = Carve()
        rq = ra[:, 0:4 * T].rearrange("p (a b) -> p a b", b=T)
        rk, rv, rg = cr(4, T), cr(4, T), cr(4, T)
        r_cos, r_sin = cr(T), cr(T)
        r_tab = region_b[:, cr.at - 2 * T:cr.at]
        t_raw, t_cos, t_rot = cr(2, T), cr(2, T), cr(2, T)
        r_dmask, r_gam, r_qdec, r_kdec = cr(4, P), cr(4, P), cr(4, P), cr(4)
        r_con = region_b[:, cr.at - 3 * 512 - 4:cr.at]
        k_st, v_st, q_st, q_dec, sc_sb, k_tm, v_tm = (cr(4, P) for _ in range(7))
        st0, st1, st_s, st_t = (cr(4, P) for _ in range(4))
        cw = Carve()
        a_kk = ra[:, 0:4 * TX].rearrange("p (a b) -> p a b", b=TX)
        a_r, a_k, a_v = (cw(4, TX) for _ in range(3))
        xwa, xg = cw(TX), cw(TX)
        pt = cw(2, TX + 1)
        d_t = cw(TX)
        shift_out = cw(28)
        cs = Carve()
        cs.at = cw.at
        qi = ra[:, 0:2 * T].rearrange("p (a b) -> p a b", b=T)
        gate_out = ra[:, 2 * T:4 * T].rearrange("p (a b) -> p a b", b=T)
        kd = cs(2, T + TP)
        ki = cs(T + TP)
        v_new, v_old = cs(5, P), cs(4, P)
        wi = cs(5, 4)
        k_rope, v_ch = cs(T), cs(T)
        top8 = cs(8)
        prob_t = cs(2, 512)
        stat = cs(2, 4)
        s_at = cs.at
        s_cos, s_sin = cs(T), cs(T)
        s_tab = region_b[:, cs.at - 2 * T:cs.at]
        s_raw, s_tcos, s_trot = cs(2, T), cs(2, T), cs(2, T)
        cs.at = s_at
        relu_sb = cs(2, T)
        score, bias = cs(T), cs(T)
        logit, prob = cs(2, T), cs(2, T)
        a_b = cw(4, TX)
        cum = cw(4, NC * 65)
        lora_g = cw(512)
        w_at = cw.at
        lora_wa = cw(512)
        lw, cmask = cw(NC * 65), cw(NC * 65)
        sq_t, clamped = cw(TX), cw(4, TX)
        Z0, Z1 = cw(256), cw(256)
        cw.at = w_at
        be, ka, LT, XX = (cw(512) for _ in range(4))
        BT, M1 = ka, be
        R_sb, U_sb, z_t = (cw(256) for _ in range(3))
        w_ends = [cw(8), cw(8)]
        sets = [[region_c[:, (9 * i + n) * 512:(9 * i + n + 1) * 512] for n in range(9)] for i in range(2)]
        al, rh, LkT, TbT, TkT, Vt, kat, bet, XT = sets[0]
        v_stage, w_end = TkT, w_ends[0]
        cp = Carve()
        cp.at = w_at
        p_sq, p_rs, p_rk, p_bv, p_y = (cp(TX) for _ in range(5))
        gate_in = ysa[:, 0:3, :]
        merged = yret[:, 0:2, :]
        gated = yret[:, 2:4, :]
        relu_m = yret[:, 0:2, :]
        sq_m = yret[:, 2:4, :]

        dense = [ctx.enter_context(nc.psum_tensor(f"dense{i}", [P, 1024], F32)) for i in range(2)]
        mix = [ctx.enter_context(nc.psum_tensor(f"mix{i}", [P, 1024], F32)) for i in range(2)]
        bank = [mix[0][:, 0:512], mix[0][:, 512:1024], mix[1][:, 0:512], mix[1][:, 512:1024]]

        gate_dram = nc.dram_tensor("gate_scratch", (N_GATE, P, T), F32, kind="Internal").ap()

        in_x, in_const, in_par = sem("in_x"), sem("in_const"), sem("in_par")
        in_ret, in_sa, in_rw, in_g2 = sem("in_ret"), sem("in_sa"), sem("in_rw"), sem("in_g2")
        gate_stored = [sem("gate_stored0"), sem("gate_stored1")]
        in_gate = [sem(f"in_gate{i}") for i in range(3)]
        gate_ready, out_stored = sem("gate_ready"), sem("out_stored")
        w_loaded = [sem(f"w_loaded{i}") for i in range(RAW)]
        w_high, w_split, w_used = sem("w_high"), sem("w_split"), sem("w_used")
        dense_free = [sem("dense_free0"), sem("dense_free1")]
        sq_ready, ssq_ready, rs_ready, act_ready = sem("sq_ready"), sem("ssq_ready"), sem("rs_ready"), sem("act_ready")
        rope_raw, rope_rot, rope_done = sem("rope_raw"), sem("rope_rot"), sem("rope_done")
        ret_sig = sem("ret_sig")
        ret_pe = Steps(sem("ret_pe"), ["turned", "gram", "state"])
        ret_dve = Steps(sem("ret_dve"), ["staged", "k_tm", "scores"])
        ret_act = Steps(sem("ret_act"), ["v_tm", "out"])
        ret_cross, ret_state = sem("ret_cross"), sem("ret_state")
        post_act = Steps(sem("post_act"), ["sq0", "sq1", "rs0", "sq2", "rs1", "sq3", "rs2", "rs3"])
        post_pe, post_dve = sem("post_pe"), sem("post_dve")
        sa_v, sa_pe, sa_act, sa_dve = sem("sa_v"), sem("sa_pe"), sem("sa_act"), sem("sa_dve")
        ix_pe, ix_act, ix_dve = sem("ix_pe"), sem("ix_act"), sem("ix_dve")
        at_scores, at_logits, at_exp, at_probs = sem("at_scores"), sem("at_logits"), sem("at_exp"), sem("at_probs")
        at_pe = Steps(sem("at_pe"), ["turned", "values"])
        at_act = Steps(sem("at_act"), ["turned", "out"])
        shift_act, shift_dve = sem("shift_act"), sem("shift_dve")
        lora_act = Steps(sem("lora_act"), ["squash"] + [f"{s}{j}" for j in range(4) for s in ("sig", "sq")]
                         + [f"norm{j}" for j in range(4)])
        lora_pe = Steps(sem("lora_pe"), [f"{s}{j}" for j in range(4) for s in ("lora", "ssq")])
        lora_dve = Steps(sem("lora_dve"), [f"{s}{j}" for j in range(4) for s in ("kk0_", "clamp")]
                         + [f"kk{j}" for j in range(4)])
        last = len(LEVELS) - 1
        rw_pe = Steps(sem("rw_pe"), ["gram", "turned"] + [f"{s}{n}" for n in range(last + 1) for s in ("m1_", "x_")])
        rw_act = Steps(sem("rw_act"), ["exp", "lt", "turned"] + [f"m1_{n}" for n in range(last + 1)])
        rw_dve = Steps(sem("rw_dve"), ["staged", "gram", "turned"]
                       + [f"{s}{n}" for n in range(last + 1) for s in ("b_", "x_")])
        ch_pe = Steps(sem("ch_pe"), ["r", "u", "y", "z"])
        ch_act = Steps(sem("ch_act"), ["r", "u", "y"])
        ch_z, lw_clear = sem("ch_z"), sem("lw_clear")
        gn_pe = Steps(sem("gn_pe"), ["mean", "var", "bonus", "gate"])
        gn_act = Steps(sem("gn_act"), ["sq", "rs"])
        gn_dve = Steps(sem("gn_dve"), ["yc", "rk", "mid", "out"])
        br_split, br_gated, mlp_act, mlp_split, fin = (
            sem("br_split"), sem("br_gated"), sem("mlp_act"), sem("mlp_split"), sem("fin"))

        waited_pe, waited_dve, waited_pool = sem("waited_pe"), sem("waited_dve"), sem("waited_pool")

        block = ctx.enter_context(nc.Block())
        R5, C9 = 5, NC
        OUTS = 8 * 16

        def pr(name, i):
            at = PARAMS[name][0] + i
            return par[:, at:at + 1]

        def out_of(ps):
            return ps.rearrange("p (a b) -> p a b", b=512)[:, :, 0:HALF]

        def halves(t):
            return t.rearrange("p (a b) -> p a b", b=HALF)

        def cum_view(lo, c0, nch):
            return cum.rearrange("p j (c t) -> p j c t", t=65)[:, :, bass.ds(c0, nch), lo:lo + C]

        def blocks3(t, n):
            return t[:, 0:n * C].rearrange("p (g t) -> p g t", t=C)

        def mask3(m, n):
            return masks[:, m, :].unsqueeze(1).broadcast_to([P, n, C])

        @block.sync
        def _(sp):
            sp.dma_start(x[:, :, :], dr["x"]).then_inc(in_x, 16)
            sp.dma_start(cst[:, :], dr["cst"]).then_inc(in_const, 16)
            sp.dma_start(masks[:, :, :], dr["masks"]).then_inc(in_const, 16)
            sp.dma_start(small[:, :], dr["small"]).then_inc(in_const, 16)
            for s in range(RAW):
                sp.dma_start(w_raw[:, s, :], dr["stream"][s]).then_inc(w_loaded[s], 16)
            with sp.Fori(1, DEPTH * NT // RAW) as g:
                for s in range(RAW):
                    sp.wait_ge(w_split, (g - 1) * RAW + s + 1)
                    sp.dma_start(w_raw[:, s, :],
                                 dr["stream"][bass.ds(g * RAW + s, 1), :, :].rearrange("a p n -> p (a n)")
                                 ).then_inc(w_loaded[s], 16)

        @block.gpsimd
        def _(pool):
            def split(g, s, used):
                v = s % SPLIT
                pool.wait_ge(w_loaded[s], g * 16 + 16)
                if used is not None:
                    pool.wait_ge(w_used, used)
                if used is not None:
                    pool.sem_inc(waited_pool, 1)
                nc.gpsimd.tensor_scalar(w_hi[:, v, :], w_raw[:, s, :], 1.0, 1.0, ALU.mult,
                                        ALU.mult).then_inc(w_high, 1)
                pool.wait_ge(w_high, g * RAW + s + 1)
                nc.gpsimd.tensor_tensor(w_lo[:, v, :], w_raw[:, s, :], w_hi[:, v, :].bitcast(F32),
                                        ALU.subtract).then_inc(w_split, 1)

            for s in range(RAW):
                split(0, s, 2 * (s - SPLIT + 1) if s >= SPLIT else None)
            with pool.Fori(1, DEPTH * NT // RAW) as g:
                for s in range(RAW):
                    split(g, s, g * (2 * RAW) + 2 * (s - SPLIT + 1))

        @block.tensor
        def _(pe):
            def acc(out, lhsT, rhs, start, stop):
                return nc.tensor.matmul(out, lhsT, rhs, start=start, stop=stop, skip_group_check=True)

            def wide(out, lhsT, rhs, width, start=True, stop=True):
                acc(out[:, 0:512], lhsT, rhs[:, 0:512], start, stop)
                return acc(out[:, 512:width], lhsT, rhs[:, 512:width], start, stop)

            def dense_slice(buf, slot, hi, lo, w_k, x_k, first, stop):
                wh, wl = (w[:, slot, w_k * P:w_k * P + P] for w in (w_hi, w_lo))
                parts = [(slice(512 * i, 512 * i + HALF), slice(HALF * i, HALF * i + HALF)) for i in range(2)]
                for out, tok in parts:
                    acc(buf[:, out], wh, hi[:, x_k, tok], first, False)
                    acc(buf[:, out], wh, lo[:, x_k, tok], False, False)
                for out, tok in parts:
                    mm = acc(buf[:, out], wl, hi[:, x_k, tok], False, stop)
                return mm

            def dense_tile(slot, buffer, split_count, free_count, hi, lo, k0=0, ks=KT, half=0, fresh=None, used=2):
                buf = dense[buffer]
                pe.wait_ge(w_split, split_count)
                pe.wait_ge(dense_free[buffer], free_count)
                for k in range(ks):
                    if fresh:
                        fresh(k)
                    mm = dense_slice(buf, slot, hi, lo, half * ks + k, k0 + k, k == 0, k == ks - 1)
                mm.then_inc(w_used, used)

            def tile(l, t, u, hi, lo, **kw):
                dense_tile(t % SPLIT, u % 2, l * NT + t + 1, free_before(u, l), hi, lo,
                           used=1 if kw.get("ks") == 4 else 2, **kw)

            def fill(l, slices):
                for s in range(*slices):
                    t, k = T_RW + s // KT, s % KT
                    buf, slot = dense[t % 2], t % SPLIT
                    if k == 0:
                        pe.wait_ge(w_split, l * NT + t + 1)
                        pe.wait_ge(dense_free[t % 2], free_before(t, l))
                    mm = dense_slice(buf, slot, act_hi, act_lo, k, k, k == 0, k == KT - 1)
                    if k == KT - 1:
                        mm.then_inc(w_used, 4 if t == T_SPARE - 1 else 2)

            def sum_squares(n):
                for k in range(KT):
                    pe.wait_ge(sq_ready, n * KT + k + 1)
                    wide(mix[0], ones, n_sq[:, k % 2, :], T, k == 0, k == KT - 1).then_inc(ssq_ready, 1)

            def rotate(l, n, mat, src):
                pe.wait_ge(rope_raw, l * 16 + n + 1)
                if n >= 2:
                    pe.wait_ge(rope_done, l * 16 + n - 1)
                wide(mix[n % 2], mat, src[:, n % 2, :], T).then_inc(rope_rot, 1)

            def retention_step(l, i, n, s_in, s_mid):
                run, ch = l * R5 + i, l * C9 + 2 * i
                chunks = n // C
                pe.wait_ge(ret_dve.sem, ret_dve.at("staged", run))
                passed()
                for h in range(4):
                    nc.tensor.transpose(bank[0][0:n, h * P:(h + 1) * P], k_st[:, h, 0:n], ident)
                for h in range(4):
                    mm = nc.tensor.transpose(bank[1][0:n, h * P:(h + 1) * P], v_st[:, h, 0:n], ident)
                mm.then_inc(ret_pe.sem, 1)
                for h in range(4):
                    mm = acc(bank[2][0:n, h * P:h * P + n], k_st[:, h, 0:n], q_st[:, h, 0:n], True, True)
                mm.then_inc(ret_pe.sem, 1)
                pe.wait_ge(ret_dve.sem, ret_dve.at("k_tm", run))
                pe.wait_ge(ret_act.sem, ret_act.at("v_tm", run))
                passed()
                for q in range(chunks):
                    for h in range(4):
                        mm = acc(bank[q][:, h * P:(h + 1) * P], k_tm[q * C:(q + 1) * C, h, :],
                                 v_tm[q * C:(q + 1) * C, h, :], True, True)
                mm.then_inc(ret_pe.sem, 1)
                pe.wait_ge(ret_dve.sem, ret_dve.at("scores", run))
                passed()
                for h in range(4):
                    acc(bank[3][:, h * P:h * P + n], v_tm[0:n, h, :], sc_sb[0:n, h, 0:n], h == 0, False)
                for h in range(4):
                    mm = acc(bank[3][:, h * P:h * P + C], s_in[:, h, :], q_dec[:, h, 0:C], False, chunks == 1)
                mm.then_inc(ret_cross, 1)
                if chunks == 2:
                    pe.wait_ge(ret_state, ch + 1)
                    passed()
                    for h in range(4):
                        mm = acc(bank[3][:, h * P + C:h * P + 2 * C], s_mid[:, h, :], q_dec[:, h, C:2 * C], False, True)
                    mm.then_inc(ret_cross, 1)

            def rwkv_step(l, i, nq, Z):
                run, ch = l * R5 + i, l * C9 + 2 * i
                halves = [slice(0, C), slice(C, P)]

                def per_block(out, lhsT, rhs):
                    for g in range(4 * nq):
                        for rows in halves:
                            b = slice(g * C, g * C + C)
                            mm = acc(out[rows, b], lhsT[rows, b], rhs[rows, b], True, True)
                    return mm

                pe.wait_ge(rw_dve.sem, rw_dve.at("staged", run))
                passed()
                per_block(bank[0], be, al)
                per_block(bank[1], al, be)
                per_block(bank[2], ka, al)
                per_block(bank[3], be, rh).then_inc(rw_pe.sem, 1)
                pe.wait_ge(rw_dve.sem, rw_dve.at("gram", run))
                pe.wait_ge(rw_act.sem, rw_act.at("lt", run))
                passed()
                for src, dst in ((v_stage, bank[1]), (ka, bank[2]), (be, bank[3])):
                    for g in range(4 * nq):
                        for rows in halves:
                            b = slice(g * C, g * C + C)
                            acc(dst[rows, b], src[rows, b], masks[rows, M_EYE, :], True, True)
                per_block(bank[0], ka, rh).then_inc(rw_pe.sem, 1)
                pe.wait_ge(rw_act.sem, rw_act.at("turned", run))
                for n in range(last + 1):
                    pe.wait_ge(rw_dve.sem, rw_dve.at(f"b_{n}", run))
                    passed()
                    per_block(bank[0], BT, XX).then_inc(rw_pe.sem, 1)
                    pe.wait_ge(rw_act.sem, rw_act.at(f"m1_{n}", run))
                    passed()
                    if n < last:
                        per_block(bank[1], XT, M1)
                    per_block(bank[2], M1, XT).then_inc(rw_pe.sem, 1)
                pe.wait_ge(rw_dve.sem, rw_dve.at(f"x_{last}", run))
                passed()
                for q in range(nq):
                    blocks = [(rows, slice((j * nq + q) * C, (j * nq + q + 1) * C), slice(j * C, (j + 1) * C))
                              for j in range(4) for rows in halves]
                    pe.wait_ge(ch_z, START + ch + q)
                    passed()
                    for rows, g, f in blocks:
                        acc(bank[0][rows, f], al[rows, g], Z[rows, f], True, False)
                        mm = acc(bank[0][rows, f], LkT[rows, g], Vt[rows, g], False, True)
                    mm.then_inc(ch_pe.sem, 1)
                    pe.wait_ge(ch_act.sem, ch_act.at("r", ch + q))
                    passed()
                    for rows, g, f in blocks:
                        mm = acc(bank[1][rows, f], XT[rows, g], R_sb[rows, f], True, True)
                    mm.then_inc(ch_pe.sem, 1)
                    pe.wait_ge(ch_act.sem, ch_act.at("u", ch + q))
                    passed()
                    for rows, g, f in blocks:
                        acc(bank[2][rows, f], Z[rows, f], rh[rows, g], True, False)
                        acc(bank[2][rows, f], U_sb[rows, f], TbT[rows, g], False, False)
                        mm = acc(bank[2][rows, f], Vt[rows, g], TkT[rows, g], False, True)
                    mm.then_inc(ch_pe.sem, 1)
                    for rows, g, f in blocks:
                        acc(bank[3][rows, f], kat[rows, g], Vt[rows, g], True, False)
                        mm = acc(bank[3][rows, f], bet[rows, g], U_sb[rows, f], False, True)
                    mm.then_inc(ch_pe.sem, 1)

            def passed():
                pe.sem_inc(waited_pe, 1)

            pe.wait_ge(in_const, 48)
            sum_squares(0)
            with pe.Fori(0, DEPTH) as l:
                for t in range(N_RET):
                    fresh = (lambda k: pe.wait_ge(act_ready, l * (2 * KT) + k + 1)) if t == 0 else None
                    tile(l, T_RET + t, T_RET + t, act_hi, act_lo, fresh=fresh)
                    if 1 <= t <= 8:
                        rotate(l, t - 1, rot_ret, t_raw)
                with pe.Fori(0, 4) as i:
                    retention_step(l, i, P, st0, st1)
                retention_step(l, 4, C, st_s, None)
                pe.wait_ge(ret_state, l * C9 + C9)
                for h in range(4):
                    pe.wait_ge(post_act.sem, post_act.at(f"sq{h}", l))
                    wide(mix[h % 2], ones, t_raw[:, h % 2, :], T).then_inc(post_pe, 1)

                rotary = {0: 8, 1: 9, 2: 10, 3: 11, 4: 12, 6: 13, 7: 14, 8: 15}
                for t in range(N_SA):
                    tile(l, T_SA + t, T_SA + t, act_hi, act_lo)
                    if t == 0:
                        pe.wait_ge(post_dve, l * 4 + 4)
                    if t - 1 in rotary:
                        rotate(l, rotary[t - 1], rot_sa, s_raw)
                rotate(l, 15, rot_sa, s_raw)
                pe.wait_ge(sa_v, l + 1)
                pe.wait_ge(rope_done, l * 16 + 16)
                passed()
                for src, at in ((v_ch, 0), (s_raw[:, 1, :], 2)):
                    for b in range(5):
                        n = P if b < 4 else C
                        out = bank[at][0:n, b * P:(b + 1) * P] if b < 4 else bank[at + 1][0:n, 0:P]
                        mm = nc.tensor.transpose(out, src[:, b * P:b * P + n], ident)
                mm.then_inc(sa_pe, 1)

                pe.wait_ge(sa_dve, l + 1)
                pe.wait_ge(sa_act, l + 1)
                pe.wait_ge(in_sa, l * 128 + 128)
                for b in range(5):
                    n, t0 = (P if b < 4 else C), b * P
                    keys = (b + 1) * P if b < 4 else T
                    nb = (keys + P - 1) // P

                    def against(out, lhsT, keys_t, half):
                        rows = slice(half * C, half * C + C)
                        if b < 4:
                            return acc(out[0:n, 0:keys], lhsT, keys_t[rows, 0:keys], True, True)
                        acc(out[0:n, 0:512], lhsT, keys_t[rows, T:T + TP], True, True)
                        return acc(out[0:n, 512:T], lhsT, keys_t[rows, TP:T], True, True)

                    if b:
                        pe.wait_ge(at_act.sem, at_act.at("out", (l * 5 + b - 1) * 8 + 7))
                        passed()
                        for i in range(4):
                            if i >= 2:
                                pe.wait_ge(ix_act, l * 16 + (b - 1) * 4 + i - 1)
                                passed()
                            half = i % 2
                            against(mix[half], qi[half * C:half * C + C, i // 2, t0:t0 + n], ki, half).then_inc(ix_pe, 1)
                        fill(l, fill_range(b))
                        pe.wait_ge(ix_act, l * 16 + b * 4)
                        passed()

                    def scores(h):
                        half, run = h % 2, (l * 5 + b) * 8 + h
                        if h >= 2:
                            pe.wait_ge(at_act.sem, at_act.at("out", run - 2))
                            passed()
                        against(mix[half], ysa[half * C:half * C + C, h // 2, t0:t0 + n],
                                kd[:, h // 4, :], half).then_inc(at_scores, 1)

                    scores(0)
                    for h in range(8):
                        half, run = h % 2, (l * 5 + b) * 8 + h
                        if h < 7:
                            scores(h + 1)
                        fill(l, fill_range(b, h, 0))
                        pe.wait_ge(at_probs, run + 1)
                        passed()
                        for kb in range(nb):
                            w = min(P, keys - kb * P)
                            mm = nc.tensor.transpose(mix[half][0:w, kb * n:(kb + 1) * n],
                                                     prob[0:n, half, kb * P:kb * P + w], ident[0:n, 0:n])
                        mm.then_inc(at_pe.sem, 1)
                        fill(l, fill_range(b, h, 1))
                        pe.wait_ge(at_act.sem, at_act.at("turned", run))
                        passed()
                        for kb in range(nb):
                            w = min(P, keys - kb * P)
                            vv = v_new[:, kb, :] if b < 4 else v_old[:, kb, :] if kb < 4 else v_new[:, 4, :]
                            mm = acc(mix[half][half * C:half * C + C, 768:768 + n],
                                     vv[0:w, (h // 4) * C:(h // 4) * C + C],
                                     prob_t[0:w, half, kb * n:(kb + 1) * n], kb == 0, kb == nb - 1)
                        mm.then_inc(at_pe.sem, 1)

                pe.wait_ge(in_rw, l * 48 + 48)
                pe.wait_ge(lora_act.sem, lora_act.at("squash", l))
                passed()
                for j in range(4):
                    if j:
                        pe.wait_ge(lora_dve.sem, lora_dve.at(f"clamp{j - 1}", l))
                        passed()
                    wide(mix[0], lora_wa[0:C, j * P:(j + 1) * P], xwa[0:C, :], TX)
                    wide(mix[1], lora_wa[C:P, j * P:(j + 1) * P], xwa[C:P, :], TX).then_inc(lora_pe.sem, 1)
                    pe.wait_ge(lora_act.sem, lora_act.at(f"sq{j}", l))
                    wide(mix[0], blk, sq_t, TX).then_inc(lora_pe.sem, 1)
                with pe.Fori(0, 4) as i:
                    rwkv_step(l, i, 2, Z0)
                rwkv_step(l, 4, 1, Z1)

                pe.wait_ge(in_g2, l * 16 + 16)
                pe.wait_ge(ch_z, START + l * C9 + C9)
                pe.wait_ge(ch_act.sem, ch_act.at("y", l * C9 + C9 - 1))
                for j in range(4):
                    run = l * 4 + j
                    if j:
                        pe.wait_ge(gn_dve.sem, gn_dve.at("out", run - 1))
                    wide(mix[0], blk, a_kk[:, j, :], TX).then_inc(gn_pe.sem, 1)
                    pe.wait_ge(gn_act.sem, gn_act.at("sq", run))
                    wide(mix[1], blk, p_sq, TX).then_inc(gn_pe.sem, 1)
                    pe.wait_ge(gn_dve.sem, gn_dve.at("rk", run))
                    wide(mix[0], blk, p_rk, TX).then_inc(gn_pe.sem, 1)
                    pe.wait_ge(gn_act.sem, gn_act.at("rs", run))
                    wide(mix[1], lora_g[:, j * P:(j + 1) * P], xg, TX).then_inc(gn_pe.sem, 1)

                for mp in range(4):
                    for b in range(3):
                        for mi in range(2):
                            n = (mp * 3 + b) * 2 + mi
                            fresh = (lambda k, b=b: pe.wait_ge(br_split, l * 12 + b * 4 + k + 1)) \
                                if mp == 0 and mi == 0 else None
                            tile(l, T_BR + mp * 3 + b, U_BR + n, in_hi, in_lo, k0=b * 4, ks=4, half=mi, fresh=fresh)
                for m in range(KT):
                    fresh = (lambda k: pe.wait_ge(br_gated, l * KT + k + 1)) if m == 0 else None
                    tile(l, T_WO + m, U_WO + m, act_hi, act_lo, fresh=fresh)
                sum_squares(l * 2 + 1)
                with pe.Fori(0, FF) as c:
                    for m in range(2 * KT):
                        up = m < KT
                        fresh = None
                        if m == 0:
                            fresh = lambda k: pe.wait_ge(act_ready, l * (2 * KT) + KT + k + 1)
                        if m == KT:
                            fresh = lambda k: pe.wait_ge(mlp_split, START + l * (FF * KT) + c * KT + k + 1)
                        dense_tile(m % SPLIT, m % 2, l * NT + T_MLP + c * (2 * KT) + m + 1,
                                   free_before(U_MLP + m, l) + c * KT,
                                   act_hi if up else in_hi, act_lo if up else in_lo, fresh=fresh)
                sum_squares(l * 2 + 2)

        @block.scalar
        def _(act):
            def op(out, in_, func, **kw):
                return nc.scalar.activation(out, in_, func, **kw)

            def taken(l, u, t, half=0):
                act.wait_ge(w_used, used_after(t, l, half))
                return out_of(dense[u % 2])

            def squares(n, waits):
                for k in range(KT):
                    waits(k)
                    if k >= 2:
                        act.wait_ge(ssq_ready, n * KT + k - 1)
                    op(n_sq[:, k % 2, :], x[:, k, :], ACT.Square).then_inc(sq_ready, 1)

            def root(out, ps, width, scale, eps_col):
                op(out, ps[:, 0:width], ACT.Ln, scale=scale, bias=small[:, eps_col:eps_col + 1])
                nc.scalar.drain()
                return op(out, out, ACT.Exp, scale=-0.5)

            def norm_root(n):
                nc.scalar.preload_act_table_set(EXP_LN)
                act.wait_ge(ssq_ready, n * KT + KT)
                root(n_rs, mix[0], T, 1.0 / D, 0).then_inc(rs_ready, 1)

            def after_dve(l, u0):
                return lambda k: act.wait_ge(dense_free[(u0 + k) % 2], free_before(u0 + k, l) + 1)

            def retention_step(l, i, n):
                run, ch = l * R5 + i, l * C9 + 2 * i
                act.wait_ge(ret_pe.sem, ret_pe.at("turned", run))
                op(v_tm[0:n], bank[1][0:n, :].rearrange("p (h e) -> p h e", e=P), ACT.Copy).then_inc(ret_act.sem, 1)
                act.wait_ge(ret_cross, START + ch + n // C)
                op(yret[:, :, bass.ds(i * P, n)], bank[3][:, :].rearrange("p (h t) -> p h t", t=P)[:, :, 0:n],
                   ACT.Copy).then_inc(ret_act.sem, 1)

            def rwkv_step(l, i, nq):
                run, ch = l * R5 + i, l * C9 + 2 * i
                w = 4 * nq * C
                c0 = i * 2
                view = lambda t: t[:, 0:w].rearrange("p (j c t) -> p j c t", j=4, t=C)
                act.wait_ge(ch_z, START + ch)
                op(view(ka), cum_view(1, c0, nq), ACT.Exp, scale=DECAY)
                op(view(al), cum_view(0, c0, nq), ACT.Exp, scale=-DECAY)
                op(view(rh), cum_view(1, c0, nq), ACT.Exp, scale=-DECAY).then_inc(rw_act.sem, 1)
                act.wait_ge(rw_pe.sem, rw_pe.at("gram", run))
                op(LT[:, 0:w], bank[0][:, 0:w], ACT.Copy).then_inc(rw_act.sem, 1)
                act.wait_ge(rw_pe.sem, rw_pe.at("turned", run))
                op(Vt[:, 0:w], bank[1][:, 0:w], ACT.Copy)
                op(kat[:, 0:w], bank[2][:, 0:w], ACT.Copy)
                op(bet[:, 0:w], bank[3][:, 0:w], ACT.Copy).then_inc(rw_act.sem, 1)
                for n in range(last + 1):
                    act.wait_ge(rw_pe.sem, rw_pe.at(f"m1_{n}", run))
                    op(M1[:, 0:w], bank[0][:, 0:w], ACT.Copy).then_inc(rw_act.sem, 1)
                for q in range(nq):
                    act.wait_ge(ch_pe.sem, ch_pe.at("r", ch + q))
                    op(R_sb, bank[0][:, 0:256], ACT.Copy).then_inc(ch_act.sem, 1)
                    act.wait_ge(ch_pe.sem, ch_pe.at("u", ch + q))
                    op(U_sb, bank[1][:, 0:256], ACT.Copy, scale=-1.0).then_inc(ch_act.sem, 1)
                    act.wait_ge(ch_pe.sem, ch_pe.at("y", ch + q))
                    t0 = i * P + q * C if nq == 2 else SX
                    op(a_kk[:, :, bass.ds(t0, C)], bank[2][:, 0:256].rearrange("p (j t) -> p j t", t=C),
                       ACT.Copy).then_inc(ch_act.sem, 1)

            for s in (*dense_free, ret_cross, ch_z, mlp_split):
                act.sem_inc(s, START)
            act.wait_ge(in_x, 16)
            squares(0, lambda k: None)
            with act.Fori(0, DEPTH) as l:
                act.dma_start(par[:, :], layer_of(dr["par"], l)).then_inc(in_par, 16)
                act.dma_start(r_tab, dr["r_tab"]).then_inc(in_ret, 16)
                act.dma_start(r_con, dr["r_con"]).then_inc(in_ret, 16)
                act.dma_start(st_s[:, :, :], layer_of(dr["st_ret"], l).rearrange("p (h e) -> p h e", e=P)).then_inc(in_ret, 16)
                act.wait_ge(in_const, 48)
                norm_root(l * 2)
                for t in range(N_RET):
                    if t < 8 and t >= 2:
                        act.wait_ge(rope_done, l * 16 + t - 1)
                    buf = taken(l, T_RET + t, T_RET + t)
                    free = dense_free[t % 2]
                    if t < 8:
                        op(halves(t_raw[:, t % 2, :]), buf, ACT.Copy, scale=1.0 if t < 4 else RET_SCALE).then_inc(rope_raw, 1)
                        act.wait_ge(rope_raw, l * 16 + t + 1)
                        act.sem_inc(free, 1)
                    elif t < 12:
                        op(halves(rv[:, t - 8, :]), buf, ACT.Copy).then_inc(free, 1)
                    else:
                        op(halves(rg[:, t - 12, :]), buf, ACT.Sigmoid).then_inc(ret_sig, 1)
                with act.Fori(0, 4) as i:
                    retention_step(l, i, P)
                act.wait_ge(ret_state, l * C9 + 8)
                act.dma_start(layer_of(outs["st_ret_p"], l).rearrange("p (h e) -> p h e", e=P), st0[:, :, :]).then_inc(out_stored, 16)
                retention_step(l, 4, C)
                nc.scalar.drain()
                act.wait_ge(ret_state, l * C9 + 9)
                act.dma_start(layer_of(outs["st_ret_s"], l).rearrange("p (h e) -> p h e", e=P), st1[:, :, :]).then_inc(out_stored, 16)
                nc.scalar.preload_act_table_set(EXP_LN)

                def post_sq(h):
                    if h >= 2:
                        act.wait_ge(post_pe, l * 4 + h - 1)
                    op(t_raw[:, h % 2, :], yret[:, h, :], ACT.Square).then_inc(post_act.sem, 1)

                def post_rs(h):
                    act.wait_ge(post_pe, l * 4 + h + 1)
                    if h >= 2:
                        act.wait_ge(post_dve, l * 4 + h - 1)
                    root(t_cos[:, h % 2, :], mix[h % 2], T, 1.0 / P, 0).then_inc(post_act.sem, 1)

                for name in post_act.names:
                    (post_sq if name.startswith("sq") else post_rs)(int(name[-1]))

                act.wait_ge(post_dve, l * 4 + 4)
                act.wait_ge(out_stored, l * OUTS + 32)
                act.dma_start(s_tab, dr["s_tab"]).then_inc(in_sa, 16)
                for kv in range(2):
                    for half in range(2):
                        act.dma_start(kd[half * C:half * C + C, kv, T:T + TP],
                                      layer_of(dr["k_old"], l)[kv * C:kv * C + C, :]).then_inc(in_sa, 16)
                for half in range(2):
                    act.dma_start(ki[half * C:half * C + C, T:T + TP], layer_of(dr["ik_old"], l)).then_inc(in_sa, 16)
                act.dma_start(v_old[:, :, :], layer_of(dr["v_old"], l).rearrange("p (b e) -> p b e", e=P)).then_inc(in_sa, 16)
                rotary = {0: 8, 1: 9, 2: 10, 3: 11, 4: 12, 6: 13, 7: 14, 8: 15}
                for t in range(N_SA):
                    u = T_SA + t
                    n = rotary.get(t)
                    if n is not None:
                        act.wait_ge(rope_done, l * 16 + n - 1)
                    buf = taken(l, u, u)
                    if n is not None:
                        op(halves(s_raw[:, n % 2, :]), buf, ACT.Copy).then_inc(rope_raw, 1)
                        act.wait_ge(rope_raw, l * 16 + n + 1)
                    else:
                        op(halves(v_ch), buf, ACT.Copy).then_inc(sa_v, 1)
                        act.wait_ge(sa_v, l + 1)
                        act.dma_start(layer_of(outs["v_new"], l), v_ch).then_inc(out_stored, 16)
                    act.sem_inc(dense_free[u % 2], 1)
                act.wait_ge(rope_done, l * 16 + 16)
                act.dma_start(layer_of(outs["k_new"], l), k_rope).then_inc(out_stored, 16)
                act.dma_start(layer_of(outs["ik_new"], l), ki[0:C, 0:T]).then_inc(out_stored, 16)
                act.wait_ge(sa_pe, l + 1)
                op(v_new[:, 0:4, :], bank[0].rearrange("p (b e) -> p b e", e=P), ACT.Copy)
                op(v_new[0:C, 4, :], bank[1][0:C, 0:P], ACT.Copy).then_inc(sa_act, 1)
                nc.scalar.preload_act_table_set(EXP_LN)

                def filled(tiles):
                    for f in tiles:
                        u = T_RW + f
                        buf = taken(l, u, u)
                        if f < N_RW:
                            if f >= 2:
                                act.wait_ge(shift_dve, l * N_RW + f - 1)
                            op(pt[:, f % 2, 1:HALF + 1], buf[:, 0, :], ACT.Copy)
                            op(pt[:, f % 2, HALF + 1:TP + 1], buf[:, 1, 0:TP - HALF], ACT.Copy)
                            op(pt[:, f % 2, TP + 1:TP + 2], pr("shift", f), ACT.Copy)
                            op(pt[:, f % 2, TP + 2:TX + 1], buf[:, 1, TP - HALF:HALF], ACT.Copy).then_inc(shift_act, 1)
                            act.wait_ge(shift_act, l * N_RW + f + 1)
                            act.sem_inc(dense_free[u % 2], 1)
                            continue
                        t = f - N_RW
                        if t >= 2:
                            act.wait_ge(gate_stored[t % 2], l * (16 * N_GATE // 2) + 16 * (t // 2))
                        op(halves(gate_out[:, t % 2, :]), buf, ACT.Copy).then_inc(dense_free[u % 2], 1)
                        act.wait_ge(dense_free[u % 2], free_before(u, l) + 1)
                        act.dma_start(gate_dram[t], gate_out[:, t % 2, :]).then_inc(gate_stored[t % 2], 16)

                for b in range(5):
                    n, t0 = (P if b < 4 else C), b * P
                    keys = (b + 1) * P if b < 4 else T
                    nb = (keys + P - 1) // P
                    if b:
                        for i in range(4):
                            at = l * 16 + (b - 1) * 4 + i
                            act.wait_ge(ix_pe, at + 1)
                            if i >= 2:
                                act.wait_ge(ix_dve, at - 1)
                            op(relu_sb[0:n, i % 2, 0:keys], mix[i % 2][0:n, 0:keys], ACT.Relu,
                               scale=IDX_SCALE).then_inc(ix_act, 1)

                    def exps(h):
                        half, run = h % 2, (l * 5 + b) * 8 + h
                        act.wait_ge(at_logits, run + 1)
                        if h >= 2:
                            act.wait_ge(at_pe.sem, at_pe.at("turned", run - 2))
                        op(prob[0:n, half, 0:keys], logit[0:n, half, 0:keys], ACT.Exp,
                           bias=stat[0:n, half, 1:2], accum_out=stat[0:n, half, 2:3]).then_inc(at_exp, 1)

                    filled(fill_done(b))
                    exps(0)
                    for h in range(8):
                        half, run = h % 2, (l * 5 + b) * 8 + h
                        if h < 7:
                            exps(h + 1)
                        filled(fill_done(b, h, 0))
                        act.wait_ge(at_pe.sem, at_pe.at("turned", run))
                        if b < 4:
                            op(prob_t[:, half, 0:nb * n], mix[half][:, 0:nb * n], ACT.Copy).then_inc(at_act.sem, 1)
                        else:
                            op(prob_t[:, half, 0:4 * n], mix[half][:, 0:4 * n], ACT.Copy)
                            op(prob_t[0:C, half, 4 * n:5 * n], mix[half][0:C, 4 * n:5 * n], ACT.Copy).then_inc(at_act.sem, 1)
                        filled(fill_done(b, h, 1))
                        act.wait_ge(at_pe.sem, at_pe.at("values", run))
                        rows = slice(half * C, half * C + C)
                        op(ysa[rows, h // 2, t0:t0 + n], mix[half][rows, 768:768 + n], ACT.Copy).then_inc(at_act.sem, 1)

                nc.scalar.drain()
                act.wait_ge(out_stored, l * OUTS + 80)
                act.dma_start(lora_wa, layer_of(dr["lora_wa"], l)).then_inc(in_rw, 16)
                act.dma_start(lora_g, layer_of(dr["lora_g"], l)).then_inc(in_g2, 16)
                act.dma_start(cmask, dr["cmask"]).then_inc(in_rw, 16)
                act.dma_start(Z1, layer_of(dr["st_rw"], l)).then_inc(in_rw, 16)
                act.wait_ge(shift_dve, l * N_RW + N_RW)
                act.dma_start(layer_of(outs["shift"], l), shift_out).then_inc(out_stored, 16)
                op(xg, xg, ACT.Sigmoid)
                op(xwa[0:C, :], xwa[0:C, :], ACT.Tanh).then_inc(lora_act.sem, 1)
                for j in range(4):
                    act.wait_ge(lora_pe.sem, lora_pe.at(f"lora{j}", l))
                    lwv = lw.rearrange("p (c t) -> p c t", t=65)[:, :, 1:65]
                    if j:
                        act.wait_ge(lora_dve.sem, lora_dve.at(f"kk0_{j - 1}", l))
                    else:
                        act.wait_ge(lw_clear, l + 1)
                    op(lwv[:, 0:8, :], mix[0][:, 0:TP].rearrange("p (c t) -> p c t", t=C), ACT.Sigmoid, bias=pr("w0", j))
                    op(lwv[:, 8, :], mix[0][:, SX:TX], ACT.Sigmoid, bias=pr("w0", j))
                    op(a_b[:, j, :], mix[1][:, 0:TX], ACT.Sigmoid, bias=pr("a0", j)).then_inc(lora_act.sem, 1)
                    act.wait_ge(lora_dve.sem, lora_dve.at(f"kk0_{j}", l))
                    op(sq_t, a_kk[:, j, :], ACT.Square).then_inc(lora_act.sem, 1)
                nc.scalar.preload_act_table_set(EXP_LN)
                act.wait_ge(lora_dve.sem, lora_dve.at("clamp3", l))
                op(clamped[:, :, :], clamped[:, :, :], ACT.Ln, scale=2.0 ** 24)
                nc.scalar.drain()
                for j in range(4):
                    op(clamped[:, j, :], clamped[:, j, :], ACT.Exp, scale=-0.5, bias=small[:, 2:3]).then_inc(lora_act.sem, 1)
                act.wait_ge(lora_dve.sem, lora_dve.at("kk3", l))
                act.wait_ge(out_stored, l * OUTS + 96)
                with act.Fori(0, 4) as i:
                    rwkv_step(l, i, 2)
                act.wait_ge(ch_z, START + l * C9 + 8)
                act.dma_start(layer_of(outs["st_rw_p"], l), Z0).then_inc(out_stored, 16)
                rwkv_step(l, 4, 1)
                act.wait_ge(ch_z, START + l * C9 + 9)
                act.dma_start(layer_of(outs["st_rw_s"], l), Z1).then_inc(out_stored, 16)
                for j in range(4):
                    run = l * 4 + j
                    act.wait_ge(gn_dve.sem, gn_dve.at("yc", run))
                    op(p_sq, p_y, ACT.Square).then_inc(gn_act.sem, 1)
                    act.wait_ge(gn_pe.sem, gn_pe.at("var", run))
                    root(p_rs, mix[1], TX, 1.0 / C, 1).then_inc(gn_act.sem, 1)
                for p in range(2):
                    act.wait_ge(gate_stored[p], (l + 1) * (16 * N_GATE // 2))
                act.wait_ge(br_split, l * 12 + 8)
                def load_gate(n):
                    mp, b, mi = n // 6, n // 2 % 3, n % 2
                    if n >= 3:
                        u = U_BR + n - 3
                        act.wait_ge(dense_free[u % 2], free_before(u, l) + 1)
                    act.dma_start(gate_in[:, n % 3, :], gate_dram[b * KT + mp * 2 + mi]).then_inc(in_gate[n % 3], 16)

                for n in range(2):
                    load_gate(n)
                for n in range(24):
                    if n + 2 < 24:
                        load_gate(n + 2)
                    act.wait_ge(in_gate[n % 3], l * 128 + 16 * (n // 3) + 16)
                    op(gate_in[:, n % 3, :], gate_in[:, n % 3, :], ACT.Sigmoid).then_inc(gate_ready, 1)
                squares(l * 2 + 1, after_dve(l, U_WO))
                norm_root(l * 2 + 1)
                with act.Fori(0, FF) as c:
                    for m in range(KT):
                        act.wait_ge(w_used, used_after(T_MLP + m, l) + c * (4 * KT))
                        if m >= 2:
                            act.wait_ge(mlp_split, START + l * (FF * KT) + c * KT + m - 1)
                        else:
                            act.wait_ge(mlp_split, START + l * (FF * KT) + c * KT)
                        op(halves(relu_m[:, m % 2, :]), out_of(dense[m % 2]), ACT.Relu).then_inc(dense_free[m % 2], 1)
                        nc.scalar.drain()
                        op(sq_m[:, m % 2, :], relu_m[:, m % 2, :], ACT.Square).then_inc(mlp_act, 1)
                squares(l * 2 + 2, after_dve(l, U_MLP + (FF - 1) * 2 * KT + KT))
            norm_root(2 * DEPTH)
            act.wait_ge(fin, KT)
            act.dma_start(outs["y"], x[:, :, :]).then_inc(out_stored, 16)
            act.wait_ge(out_stored, DEPTH * OUTS + 16)

        @block.vector
        def _(dve):
            v = nc.vector

            def settle():
                v.drain()

            def passed():
                dve.sem_inc(waited_dve, 1)

            def norm_apply(n, gain):
                dve.wait_ge(rs_ready, n + 1)
                for k in range(0, KT, 2):
                    for i in range(2):
                        v.scalar_tensor_tensor(n_t[:, i, :], x[:, k + i, :], gain(k + i), n_rs, ALU.mult, ALU.mult)
                    settle()
                    for i in range(2):
                        v.tensor_copy(act_hi[:, k + i, :], n_t[:, i, :])
                    settle()
                    for i in range(2):
                        v.tensor_tensor(act_lo[:, k + i, :], n_t[:, i, :], act_hi[:, k + i, :].bitcast(F32),
                                        ALU.subtract).then_inc(act_ready, 1)
                    settle()

            def rope(l, n, raw, tc, tr, cos, sin, dst, rows=P):
                s = slice(0, rows)
                dve.wait_ge(rope_raw, l * 16 + n + 1)
                v.tensor_tensor(tc[s, n % 2, :], raw[s, n % 2, :], cos[s], ALU.mult)
                dve.wait_ge(rope_rot, l * 16 + n + 1)
                v.tensor_tensor(tr[s, n % 2, :], mix[n % 2][s, 0:T], sin[s], ALU.mult)
                settle()
                v.tensor_tensor(dst, tc[s, n % 2, :], tr[s, n % 2, :], ALU.add).then_inc(rope_done, 1)

            def retention_step(l, i, n, s_in, s_mid, s_out):
                run, ch = l * R5 + i, l * C9 + 2 * i
                tok = bass.ds(i * P, n)
                dve.wait_ge(ret_cross, START + ch)
                v.tensor_copy(k_st[:, :, 0:n], rk[:, :, tok])
                v.tensor_copy(v_st[:, :, 0:n], rv[:, :, tok])
                v.tensor_copy(q_st[:, :, 0:n], rq[:, :, tok])
                v.tensor_tensor(q_dec[:, :, 0:n], rq[:, :, tok], r_qdec[:, :, 0:n], ALU.mult).then_inc(ret_dve.sem, 1)
                dve.wait_ge(ret_pe.sem, ret_pe.at("turned", run))
                v.tensor_tensor(k_tm[0:n], bank[0][0:n, :].rearrange("p (h e) -> p h e", e=P),
                                r_kdec[0:n].unsqueeze(2).broadcast_to([n, 4, P]), ALU.mult).then_inc(ret_dve.sem, 1)
                dve.wait_ge(ret_pe.sem, ret_pe.at("gram", run))
                v.tensor_tensor(sc_sb[0:n, :, 0:n], bank[2][0:n, :].rearrange("p (h t) -> p h t", t=P)[:, :, 0:n],
                                r_dmask[0:n, :, 0:n], ALU.mult).then_inc(ret_dve.sem, 1)
                for q, (a, z) in enumerate([(s_in, s_mid), (s_mid, s_out)][0:n // C]):
                    v.tensor_tensor(st_t[:, :, :], a[:, :, :], r_gam[:, :, :], ALU.mult)
                    settle()
                    if q:
                        dve.wait_ge(ret_cross, START + ch + 1)
                    else:
                        dve.wait_ge(ret_pe.sem, ret_pe.at("state", run))
                    v.tensor_tensor(z[:, :, :], st_t[:, :, :], bank[q].rearrange("p (h e) -> p h e", e=P),
                                    ALU.add).then_inc(ret_state, 1)
                    settle()

            def rwkv_step(l, i, nq, Z):
                run, ch = l * R5 + i, l * C9 + 2 * i
                g, w = 4 * nq, 4 * nq * C
                tok = bass.ds(i * P if nq == 2 else SX, nq * C)
                view = lambda t: t[:, 0:w].rearrange("p (j t) -> p j t", j=4)
                flat = lambda t: t[:, 0:w]
                dve.wait_ge(rw_act.sem, rw_act.at("exp", run))
                v.tensor_copy(w_end[:, 0:g], blocks3(rh, g)[:, :, C - 1])
                v.tensor_tensor(view(be), a_b[:, :, tok], view(ka), ALU.mult)
                v.tensor_tensor(view(al), a_kk[:, :, tok], view(al), ALU.mult)
                settle()
                v.tensor_tensor(view(ka), a_k[:, :, tok], view(ka), ALU.mult)
                v.tensor_tensor(view(rh), a_r[:, :, tok], view(rh), ALU.mult)
                v.tensor_copy(view(v_stage), a_v[:, :, tok]).then_inc(rw_dve.sem, 1)
                dve.wait_ge(rw_pe.sem, rw_pe.at("gram", run))
                v.tensor_tensor(blocks3(XX, g), blocks3(bank[1], g), mask3(M_PAIR_T, g), ALU.mult)
                v.tensor_tensor(blocks3(LkT, g), blocks3(bank[2], g), mask3(M_STRICT, g), ALU.mult)
                v.tensor_tensor(blocks3(TbT, g), blocks3(bank[3], g), mask3(M_INCL, g), ALU.mult).then_inc(rw_dve.sem, 1)
                dve.wait_ge(rw_act.sem, rw_act.at("lt", run))
                v.tensor_tensor(blocks3(XT, g), blocks3(LT, g), mask3(M_PAIR, g), ALU.mult)
                settle()
                v.tensor_tensor(blocks3(XX, g), mask3(M_EYE, g), blocks3(XX, g), ALU.subtract)
                v.tensor_tensor(blocks3(XT, g), mask3(M_EYE, g), blocks3(XT, g), ALU.subtract)
                dve.wait_ge(rw_pe.sem, rw_pe.at("turned", run))
                v.tensor_tensor(blocks3(TkT, g), blocks3(bank[0], g), mask3(M_INCL, g), ALU.mult).then_inc(rw_dve.sem, 1)
                for n in range(last + 1):
                    v.tensor_tensor(blocks3(BT, g), blocks3(LT, g), mask3(M_LEVEL + n, g), ALU.mult).then_inc(rw_dve.sem, 1)
                    dve.wait_ge(rw_pe.sem, rw_pe.at(f"x_{n}", run))
                    if n < last:
                        v.tensor_tensor(flat(XX), flat(XX), bank[1][:, 0:w], ALU.subtract)
                    v.tensor_tensor(flat(XT), flat(XT), bank[2][:, 0:w], ALU.subtract).then_inc(rw_dve.sem, 1)
                    settle()
                for q in range(nq):
                    dve.wait_ge(ch_pe.sem, ch_pe.at("z", ch + q))
                    v.tensor_tensor(z_t, Z, bank[3][:, 0:256], ALU.add)
                    settle()
                    decay = w_end[:, 0:g].rearrange("p (j q) -> p j q", q=nq)[:, :, q]
                    v.tensor_tensor(blocks3(Z, 4), blocks3(z_t, 4), decay.unsqueeze(2).broadcast_to([P, 4, C]),
                                    ALU.mult).then_inc(ch_z, 1)
                    settle()

            dve.wait_ge(in_x, 16)
            dve.wait_ge(in_const, 48)
            with dve.Fori(0, DEPTH) as l:
                dve.wait_ge(in_par, l * 16 + 16)
                norm_apply(l * 2, lambda k: pr("g1", k))
                dve.wait_ge(in_ret, l * 48 + 48)
                for n in range(8):
                    rope(l, n, t_raw, t_cos, t_rot, r_cos, r_sin, rq[:, n, :] if n < 4 else rk[:, n - 4, :])
                v.memset(st0[:, :, :], 0.0)
                for h in range(4):
                    u = 12 + h
                    dve.wait_ge(ret_sig, l * 4 + h + 1)
                    v.tensor_tensor(halves(rg[:, h, :]), out_of(dense[u % 2]), halves(rg[:, h, :]), ALU.mult).then_inc(dense_free[u % 2], 1)
                settle()
                with dve.Fori(0, 4) as i:
                    retention_step(l, i, P, st0, st1, st0)
                retention_step(l, 4, C, st_s, st1, None)
                for h in range(4):
                    dve.wait_ge(post_act.sem, post_act.at(f"rs{h}", l))
                    v.tensor_tensor(t_rot[:, h % 2, :], yret[:, h, :], t_cos[:, h % 2, :], ALU.mult)
                    settle()
                    v.tensor_tensor(yret[:, h, :], t_rot[:, h % 2, :], rg[:, h, :], ALU.mult).then_inc(post_dve, 1)

                dve.wait_ge(out_stored, l * OUTS + 32)
                dve.wait_ge(in_sa, l * 128 + 128)
                for n in range(8, 16):
                    rows = C if n == 15 else P
                    dst = ysa[:, n - 8, :] if n < 12 else k_rope if n == 12 else qi[:, n - 13, :] if n < 15 else ki[0:C, 0:T]
                    rope(l, n, s_raw, s_tcos, s_trot, s_cos, s_sin, dst, rows)
                settle()
                for kv in range(2):
                    for half in range(2):
                        v.tensor_copy(kd[half * C:half * C + C, kv, 0:T], k_rope[kv * C:kv * C + C])
                v.tensor_copy(ki[C:P, 0:T], ki[0:C, 0:T])
                dve.wait_ge(sa_pe, l + 1)
                v.tensor_copy(wi[:, 0:4, :], bank[2].rearrange("p (b e) -> p b e", e=P)[:, :, C:C + 4])
                v.tensor_copy(wi[0:C, 4, :], bank[3][0:C, C:C + 4]).then_inc(sa_dve, 1)
                settle()
                v.memset(pt[:, :, 0:1], 0.0)
                settle()
                shifted = [a[:, j, :] for a in (a_r, a_k, a_v) for j in range(4)] + [xwa, xg]

                def token_shift(tiles):
                    for t in tiles:
                        if t >= N_RW:
                            continue
                        cur = pt[:, t % 2, :]
                        dve.wait_ge(shift_act, l * N_RW + t + 1)
                        v.tensor_tensor(d_t, cur[:, 0:TX], cur[:, 1:TX + 1], ALU.subtract)
                        v.tensor_copy(shift_out[:, t:t + 15:14], cur[:, TP:TX + 1:65])
                        settle()
                        v.scalar_tensor_tensor(shifted[t], d_t, pr("mu", t), cur[:, 1:TX + 1], ALU.mult,
                                               ALU.add).then_inc(shift_dve, 1)
                        settle()

                for b in range(5):
                    n = P if b < 4 else C
                    keys = (b + 1) * P if b < 4 else T
                    if b == 0:
                        v.memset(bias[:, 0:P], 0.0)
                        settle()
                        v.memset(bias[0:C, C:P], NEG)
                        settle()
                    else:
                        for i in range(4):
                            dve.wait_ge(ix_act, l * 16 + (b - 1) * 4 + i + 1)
                            rel, hw = relu_sb[0:n, i % 2, 0:keys], wi[0:n, b, i:i + 1]
                            sc = score[0:n, 0:keys]
                            if i == 0:
                                v.tensor_scalar(sc, rel, hw, None, ALU.mult).then_inc(ix_dve, 1)
                            else:
                                v.scalar_tensor_tensor(sc, rel, hw, sc, ALU.mult, ALU.add).then_inc(ix_dve, 1)
                            settle()
                        if b < 4:
                            v.memset(score[0:C, keys - C:keys], FILL)
                            settle()
                        rounds = (TOPK_P if b < 4 else TOPK_S) // 8
                        with dve.Fori(0, rounds // 2):
                            for _ in range(2):
                                v.max(out=top8[0:n], in_=sc)
                                settle()
                                v.match_replace(out=sc, in_to_replace=top8[0:n], in_values=sc, imm_value=MARK)
                                settle()
                        v.tensor_scalar(bias[0:n, 0:keys], sc, EDGE, NEG, ALU.is_gt, ALU.mult)
                        settle()

                    def logits(h):
                        half, run = h % 2, (l * 5 + b) * 8 + h
                        dve.wait_ge(at_scores, run + 1)
                        if h >= 2:
                            dve.wait_ge(at_exp, run - 1)
                        passed()
                        v.tensor_tensor_reduce(logit[0:n, half, 0:keys], mix[half][0:n, 0:keys], bias[0:n, 0:keys],
                                               SA_SCALE, -3.0e38, ALU.add, ALU.max, stat[0:n, half, 0:1])
                        settle()
                        v.tensor_scalar(stat[0:n, half, 1:2], stat[0:n, half, 0:1], -1.0, None,
                                        ALU.mult).then_inc(at_logits, 1)

                    token_shift(fill_done(b))
                    logits(0)
                    for h in range(8):
                        half, run = h % 2, (l * 5 + b) * 8 + h
                        if h < 7:
                            logits(h + 1)
                        dve.wait_ge(at_exp, run + 1)
                        v.reciprocal(stat[0:n, half, 3:4], stat[0:n, half, 2:3])
                        settle()
                        v.tensor_scalar(prob[0:n, half, 0:keys], prob[0:n, half, 0:keys], stat[0:n, half, 3:4], None,
                                        ALU.mult).then_inc(at_probs, 1)
                        token_shift(fill_done(b, h, 0))
                        token_shift(fill_done(b, h, 1))

                dve.wait_ge(at_act.sem, at_act.at("out", (l * 5 + 4) * 8 + 7))
                dve.wait_ge(out_stored, l * OUTS + 80)
                for p in range(2):
                    dve.wait_ge(gate_stored[p], (l + 1) * (16 * N_GATE // 2))
                v.memset(Z0, 0.0)
                v.memset(lw, 0.0).then_inc(lw_clear, 1)
                settle()
                dve.wait_ge(in_rw, l * 48 + 48)
                for j in range(4):
                    dve.wait_ge(lora_act.sem, lora_act.at(f"sig{j}", l))
                    v.tensor_tensor_scan(cum[:, j, :], cmask, lw, 0.0, ALU.mult, ALU.add)
                    v.tensor_scalar(a_kk[:, j, :], a_k[:, j, :], pr("k_k", j), None, ALU.mult).then_inc(lora_dve.sem, 1)
                    v.tensor_scalar(d_t, a_b[:, j, :], -1.0, pr("k_a", j), ALU.add, ALU.mult)
                    settle()
                    v.scalar_tensor_tensor(a_k[:, j, :], d_t, 1.0, a_k[:, j, :], ALU.add, ALU.mult)
                    dve.wait_ge(lora_pe.sem, lora_pe.at(f"ssq{j}", l))
                    v.tensor_scalar(clamped[:, j, :], mix[0][:, 0:TX], 1e-24, None, ALU.max).then_inc(lora_dve.sem, 1)
                for j in range(4):
                    dve.wait_ge(lora_act.sem, lora_act.at(f"norm{j}", l))
                    v.tensor_tensor(a_kk[:, j, :], a_kk[:, j, :], clamped[:, j, :], ALU.mult)
                    settle()
                    v.tensor_tensor(a_b[:, j, :], a_kk[:, j, :], a_b[:, j, :], ALU.mult).then_inc(lora_dve.sem, 1)
                settle()
                dve.wait_ge(out_stored, l * OUTS + 96)
                passed()
                with dve.Fori(0, 4) as i:
                    rwkv_step(l, i, 2, Z0)
                rwkv_step(l, 4, 1, Z1)
                dve.wait_ge(out_stored, l * OUTS + OUTS)
                for j in range(4):
                    run = l * 4 + j
                    dve.wait_ge(gn_pe.sem, gn_pe.at("mean", run))
                    v.scalar_tensor_tensor(p_y, mix[0][:, 0:TX], -1.0 / C, a_kk[:, j, :], ALU.mult, ALU.add).then_inc(gn_dve.sem, 1)
                    v.scalar_tensor_tensor(p_rk, a_r[:, j, :], pr("r_k", j), a_k[:, j, :], ALU.mult, ALU.mult).then_inc(gn_dve.sem, 1)
                    dve.wait_ge(gn_pe.sem, gn_pe.at("bonus", run))
                    v.tensor_tensor(p_bv, mix[0][:, 0:TX], a_v[:, j, :], ALU.mult)
                    dve.wait_ge(gn_act.sem, gn_act.at("rs", run))
                    v.scalar_tensor_tensor(p_y, p_y, pr("lnx", j), p_rs, ALU.mult, ALU.mult).then_inc(gn_dve.sem, 1)
                    settle()
                    v.tensor_tensor(p_y, p_y, p_bv, ALU.add)
                    settle()
                    dve.wait_ge(gn_pe.sem, gn_pe.at("gate", run))
                    v.tensor_tensor(a_kk[:, j, :], mix[1][:, 0:TX], p_y, ALU.mult).then_inc(gn_dve.sem, 1)
                settle()
                for b in range(3):
                    for k in range(4):
                        if b == 0:
                            v.tensor_copy(in_hi[:, k, 0:TP], a_kk[:, k, 0:TP])
                            v.tensor_copy(in_hi[:, k, TP:T], a_kk[:, k, SX:TX])
                        else:
                            v.tensor_copy(in_hi[:, b * 4 + k, :], (ysa, yret)[b - 1][:, k, :])
                    settle()
                    for k in range(4):
                        hi = in_hi[:, b * 4 + k, :].bitcast(F32)
                        lo = in_lo[:, b * 4 + k, :]
                        if b == 0:
                            v.tensor_tensor(lo[:, 0:TP], a_kk[:, k, 0:TP], hi[:, 0:TP], ALU.subtract)
                            v.tensor_tensor(lo[:, TP:T], a_kk[:, k, SX:TX], hi[:, TP:T], ALU.subtract).then_inc(br_split, 1)
                        else:
                            v.tensor_tensor(lo, (ysa, yret)[b - 1][:, k, :], hi, ALU.subtract).then_inc(br_split, 1)
                settle()
                for n in range(24):
                    mp, b, mi = n // 6, n // 2 % 3, n % 2
                    u = U_BR + n
                    dve.wait_ge(w_used, used_after(T_BR + n // 2, l, 0 if mi else 1))
                    dve.wait_ge(gate_ready, l * 24 + n + 1)
                    ps, gate = out_of(dense[u % 2]), halves(gate_in[:, n % 3, :])
                    if b == 0:
                        v.tensor_tensor(halves(merged[:, mi, :]), ps, gate, ALU.mult).then_inc(dense_free[u % 2], 1)
                        continue
                    v.tensor_tensor(halves(gated[:, mi, :]), ps, gate, ALU.mult).then_inc(dense_free[u % 2], 1)
                    settle()
                    v.tensor_tensor(merged[:, mi, :], merged[:, mi, :], gated[:, mi, :], ALU.add)
                    settle()
                    if b == 2:
                        m = mp * 2 + mi
                        v.tensor_copy(act_hi[:, m, :], merged[:, mi, :])
                        settle()
                        v.tensor_tensor(act_lo[:, m, :], merged[:, mi, :], act_hi[:, m, :].bitcast(F32),
                                        ALU.subtract).then_inc(br_gated, 1)
                        settle()
                for m in range(KT):
                    u = U_WO + m
                    dve.wait_ge(w_used, used_after(T_WO + m, l))
                    v.tensor_tensor(halves(x[:, m, :]), halves(x[:, m, :]), out_of(dense[u % 2]), ALU.add).then_inc(dense_free[u % 2], 1)
                settle()
                norm_apply(l * 2 + 1, lambda k: pr("g2", k))
                settle()
                with dve.Fori(0, FF) as c:
                    for m in range(KT):
                        dve.wait_ge(mlp_act, l * (FF * KT) + c * KT + m + 1)
                        v.tensor_copy(in_hi[:, m, :], sq_m[:, m % 2, :])
                        settle()
                        v.tensor_tensor(in_lo[:, m, :], sq_m[:, m % 2, :], in_hi[:, m, :].bitcast(F32),
                                        ALU.subtract).then_inc(mlp_split, 1)
                    for m in range(KT):
                        dve.wait_ge(w_used, used_after(T_MLP + KT + m, l) + c * (4 * KT))
                        v.tensor_tensor(halves(x[:, m, :]), halves(x[:, m, :]), out_of(dense[m % 2]), ALU.add).then_inc(dense_free[m % 2], 1)
                    settle()
            dve.wait_ge(rs_ready, 2 * DEPTH + 1)
            for k in range(KT):
                v.scalar_tensor_tensor(x[:, k, :], x[:, k, :], small[:, 8 + k:9 + k], n_rs, ALU.mult, ALU.mult).then_inc(fin, 1)



def channel_tiles(a):
    return np.moveaxis(a.reshape(a.shape[:-1] + (-1, P)), -1, -2)


def rope_tables(width, freqs, rows, zero_rest):
    pos = np.concatenate([np.arange(TP), TP + np.arange(TS)]).astype(np.float32)
    ang = (pos[:, None] * freqs[None, :].astype(np.float32)).astype(np.float32)
    half = len(freqs)
    cos, sin = np.ones((rows, T), np.float32), np.zeros((rows, T), np.float32)
    for h in range(0, rows, width):
        for part in (0, half):
            cos[h + part:h + part + half] = np.cos(ang).T
            sin[h + part:h + part + half] = np.sin(ang).T
    return np.concatenate([cos, sin], 1)


def rotation(width, half):
    r = np.zeros((P, P), np.float32)
    for h in range(0, P, width):
        for i in range(half):
            r[h + half + i, h + i] = -1.0
            r[h + i, h + half + i] = 1.0
    return r


def constants():
    f32 = np.float32
    eye = np.eye(P, dtype=f32)
    blk = np.kron(np.eye(2, dtype=f32), np.ones((C, C), f32))
    cst = np.concatenate([eye, np.ones((P, P), f32), blk, rotation(64, 8), rotation(128, 64)], 1)
    s, t = np.meshgrid(np.arange(C), np.arange(C), indexing="ij")
    level = lambda h: (s // (2 * h) == t // (2 * h)) & (s % (2 * h) < h) & (t % (2 * h) >= h)
    m = [s < t, s <= t, level(1), level(1).T, s == t] + [level(h) for h in LEVELS]
    masks = np.stack([np.concatenate([a, a], 0) for a in m], 1).astype(f32)
    small = np.zeros((P, 16), f32)
    small[:, 0], small[:, 1], small[:, 2] = EPS, GN_EPS, 12 * np.log(2.0)
    lg = np.log1p(-np.exp2(-5.0 - np.arange(4)))
    i = np.arange(P)
    same = (i[:, None] // C) == (i[None, :] // C)
    dmask = np.exp(np.abs(i[:, None] - i[None, :])[:, None, :] * lg[None, :, None]) * same[:, None, :]
    gam = np.broadcast_to(np.exp(C * lg)[None, :, None], (P, 4, P))
    qdec = np.broadcast_to(np.exp((i % C + 1)[None, None, :] * lg[None, :, None]), (P, 4, P))
    kdec = np.exp((C - 1 - i % C)[:, None] * lg[None, :])
    r_con = np.concatenate([dmask.reshape(P, -1), gam.reshape(P, -1), qdec.reshape(P, -1), kdec], 1).astype(f32)
    sa_f = (1.0 / (500000.0 ** (np.arange(0, 16, 2, dtype=f32) / 16))).astype(f32)
    ret_f = (1.0 / (10000.0 ** np.linspace(0.0, 1.0, 64, dtype=f32))).astype(f32)
    cmask = np.ones((P, NC, 65), f32)
    cmask[:, :, 0] = 0.0
    return {"cst": cst, "masks": masks, "small": small, "r_con": r_con, "cmask": cmask.reshape(P, -1),
            "r_tab": rope_tables(128, ret_f, P, False), "s_tab": rope_tables(64, sa_f, P, True)}


def weight_tiles(w):
    n = w.shape[1] // P
    return w.reshape(KT, P, n, P).transpose(2, 1, 0, 3).reshape(n, P, KT * P)


def kernel(**inputs):
    import concourse.bacc as bacc
    from concourse.bass_utils import run_bass_kernel_spmd

    a = {k: np.asarray(v) for k, v in inputs.items()}
    arrays = constants()
    arrays["x"] = np.ascontiguousarray(
        np.concatenate([a["x_prompt"][0], a["x_sample"][0]], 0).reshape(T, KT, P).transpose(2, 1, 0))
    arrays["small"] = np.concatenate([arrays["small"][:, 0:8], channel_tiles(a["final_norm_g"])], 1)
    stream = []
    for l in range(DEPTH):
        w = a["w_in"][l]
        rw, sa, ret, gate = np.split(w, [1792, 2884, 4932], 1)
        pad = lambda m, n: np.concatenate([m, np.zeros((m.shape[0], n), m.dtype)], 1)
        stream += [weight_tiles(ret), weight_tiles(pad(sa, 60)), weight_tiles(rw), weight_tiles(pad(gate, P))]
        br = np.stack([a[n][l] for n in ("w_br_rwkv", "w_br_dsa", "w_br_ret")])
        stream.append(br.reshape(3, 4, P, 4, 2, P).transpose(3, 0, 2, 4, 1, 5).reshape(12, P, 8 * P))
        stream.append(weight_tiles(a["w_o"][l]))
        for c in range(FF):
            stream.append(weight_tiles(a["w_up"][l][:, c * D:(c + 1) * D]))
            stream.append(weight_tiles(a["w_down"][l][c * D:(c + 1) * D, :]))
    arrays["stream"] = np.ascontiguousarray(np.concatenate(stream, 0))
    cols = {"g1": a["norm1_g"], "g2": a["norm2_g"], "mu": a["rwkv_mu"], "w0": a["rwkv_w0"], "a0": a["rwkv_a0"],
            "k_k": a["rwkv_k_k"], "k_a": a["rwkv_k_a"], "r_k": a["rwkv_r_k"].reshape(DEPTH, -1),
            "lnx": a["rwkv_lnx_g"], "shift": a["state_rwkv_shift"][:, 0]}
    arrays["par"] = np.concatenate([channel_tiles(cols[n]) for n in PARAMS], 2)
    arrays["lora_wa"] = np.concatenate([a["rwkv_w2"], a["rwkv_a2"]], 1)
    arrays["lora_g"] = a["rwkv_g2"]
    arrays["st_ret"] = a["state_ret"][:, 0].transpose(0, 2, 1, 3).reshape(DEPTH, P, 512)
    arrays["st_rw"] = a["state_rwkv"][:, 0].reshape(DEPTH, 4, 2, C, C).transpose(0, 2, 4, 1, 3).reshape(DEPTH, P, 256)
    arrays["k_old"] = a["cache_dsa_k"][:, 0].reshape(DEPTH, TP, P).transpose(0, 2, 1)
    arrays["ik_old"] = a["cache_dsa_ik"][:, 0].transpose(0, 2, 1)
    arrays["v_old"] = a["cache_dsa_v"][:, 0].reshape(DEPTH, 4, P, P).transpose(0, 2, 1, 3).reshape(DEPTH, P, 512)
    arrays = {k: np.ascontiguousarray(v) for k, v in arrays.items()}

    nc = bacc.Bacc("TRN2", target_bir_lowering=False, num_devices=1)
    dr = {k: nc.dram_tensor(f"in_{k}", v.shape, mybir.dt.from_np(v.dtype), kind="ExternalInput").ap()
          for k, v in arrays.items()}
    shapes = {"y": (P, KT, T), "k_new": (DEPTH, P, T), "v_new": (DEPTH, P, T), "ik_new": (DEPTH, C, T),
              "shift": (DEPTH, P, 28), "st_rw_p": (DEPTH, P, 256), "st_rw_s": (DEPTH, P, 256),
              "st_ret_p": (DEPTH, P, 512), "st_ret_s": (DEPTH, P, 512)}
    outs = {k: nc.dram_tensor(f"out_{k}", s, F32, kind="ExternalOutput").ap() for k, s in shapes.items()}
    build(nc, dr, outs)
    r = run_bass_kernel_spmd(nc, [{f"in_{k}": v for k, v in arrays.items()}], core_ids=[0]).results[0]
    o = {k: r[f"out_{k}"] for k in shapes}

    y = o["y"].transpose(2, 1, 0).reshape(T, D)
    kv = lambda n, s: o[n][:, :, s].transpose(0, 2, 1).reshape(DEPTH, 1, -1, 2, C)
    ik = lambda s: o["ik_new"][:, :, s].transpose(0, 2, 1)[:, None]
    rw = lambda n: o[n].reshape(DEPTH, 2, C, 4, C).transpose(0, 3, 1, 4, 2).reshape(DEPTH, 1, 8, C, C)
    ret = lambda n: o[n].reshape(DEPTH, P, 4, P).transpose(0, 2, 1, 3)[:, None]
    shift = lambda i: o["shift"][:, :, 14 * i:14 * i + 14].transpose(0, 2, 1).reshape(DEPTH, 1, 1792)
    pr, sa = slice(0, TP), slice(TP, T)
    return (y[None, :TP], y[None, TP:],
            kv("k_new", pr), kv("v_new", pr), ik(pr), rw("st_rw_p"), shift(0), ret("st_ret_p"),
            kv("k_new", sa), kv("v_new", sa), ik(sa), rw("st_rw_s"), shift(1), ret("st_ret_s"))
```

```python
from contextlib import ExitStack

import numpy as np

import concourse.bass as bass
from concourse import mybir

F32 = mybir.dt.float32
F32R = mybir.dt.float32r
ALU = mybir.AluOpType
ACT = mybir.ActivationFunctionType
EXP_LN = "natural_log_exp_and_others"

P = 128
DEPTH = 2
D = 1024
KT = D // P
TP, TS = 512, 64
T = TP + TS
HALF = T // 2
TX = T + 1
SX = TP + 1
C = 64
NC = T // C
EPS = 1e-6
GN_EPS = 64e-5
DECAY = float(np.exp(-0.5))
SA_SCALE = 64 ** -0.5
IDX_SCALE = (64 ** -0.5) * (4 ** -0.5)
RET_SCALE = 128 ** -0.5
NEG = -1e30
FILL, MARK, EDGE = -3.0e38, -3.4e38, -3.2e38
TOPK_P = min(256, TP // 4)
TOPK_S = min(256, (TP + TS) // 4)
FF = 4

N_RET, N_SA, N_RW, N_GATE = 16, 9, 14, 24
T_RET = 0
T_SA = T_RET + N_RET
T_RW = T_SA + N_SA
T_GATE = T_RW + N_RW
T_SPARE = T_GATE + N_GATE
T_BR = T_SPARE + 1
T_WO = T_BR + 12
T_MLP = T_WO + KT
NT = T_MLP + FF * 2 * KT
RAW, SPLIT = 4, 2
assert NT % RAW == 0 and NT % SPLIT == 0

U_BR = T_BR
U_WO = U_BR + 24
U_MLP = U_WO + KT
NU = U_MLP + FF * 2 * KT
assert NU % 2 == 0

GATES_DSA = 6
FILL_TOPK = (0, 18, 20, 20, 22)
FILL_HEAD = (1, 1)
T_GATE_RW = T_GATE + GATES_DSA
assert GATES_DSA % 2 == 0 and sum(FILL_TOPK) + 5 * 8 * sum(FILL_HEAD) == (N_RW + GATES_DSA) * KT
STEP_CHUNKS = (2, 2, 2, 2, 1)
RW_BODIES = ((0, None), (1, 0), (2, 1), (3, 2), (4, 3), (None, 4))
BODY_STAGES = (12, 18, 18, 18, 18, 3)
BODY_SHARE = (3, 2, 2, 2, 2, 2)


def fill_range(b, h=None, part=0):
    first = sum(FILL_TOPK[:b]) + b * 8 * sum(FILL_HEAD)
    if h is None:
        return first, first + FILL_TOPK[b]
    first += FILL_TOPK[b] + h * sum(FILL_HEAD) + (FILL_HEAD[0] if part else 0)
    return first, first + FILL_HEAD[part]


def body_range(body, stage):
    total, shares = (N_GATE - GATES_DSA) * KT, [n * w for n, w in zip(BODY_STAGES, BODY_SHARE)]
    at = sum(shares[:body]) + stage * BODY_SHARE[body]
    return at * total // sum(shares), (at + BODY_SHARE[body]) * total // sum(shares)


def done(first, end):
    return range(first // KT, end // KT)


PARAMS = {}
for _name, _n in (("g1", 8), ("g2", 8), ("mu", 14), ("w0", 4), ("a0", 4), ("k_k", 4), ("k_a", 4),
                  ("r_k", 4), ("lnx", 4), ("shift", 14)):
    PARAMS[_name] = (sum(v[1] for v in PARAMS.values()), _n)
NPAR = sum(v[1] for v in PARAMS.values())

START = 1

M_STRICT, M_INCL, M_PAIR, M_PAIR_T, M_EYE, M_LEVEL = 0, 1, 2, 3, 4, 5
LEVELS = (2, 4, 8, 16, 32)
NMASK = M_LEVEL + len(LEVELS)


class Steps:

    def __init__(self, sem, runs, names):
        self.sem, self.runs, self.names = sem, runs, list(names)

    def at(self, name, layer, run=0):
        return layer * (self.runs * len(self.names)) + (run * len(self.names) + self.names.index(name) + 1)


def buffer_of(u):
    return 0 if T_GATE_RW <= u < T_SPARE else u % 2


def free_before(u, layer, back=0):
    same = [w for w in range(NU) if w != T_SPARE and buffer_of(w) == buffer_of(u)]
    return layer * len(same) + (sum(1 for w in same if w < u) + START + back)


def used_after(t, layer, half=0):
    return layer * (2 * NT) + (2 * t + (1 if half == 1 else 2))


def layer_of(t, l):
    return t[bass.ds(l, 1), :, :].rearrange("a p n -> p (a n)")


def build(nc, dr, outs):
    with ExitStack() as ctx:
        def sb(name, shape, dt=F32):
            return ctx.enter_context(nc.sbuf_tensor(name, shape, dt))

        def sem(name):
            return ctx.enter_context(nc.semaphore(name))

        x = sb("x", [P, KT, T])
        act_hi = sb("act_hi", [P, KT, T], F32R)
        act_lo = sb("act_lo", [P, KT, T], F32R)
        w_raw = sb("w_raw", [P, RAW, 1024])
        w_hi = sb("w_hi", [P, SPLIT, 1024], F32R)
        w_lo = sb("w_lo", [P, SPLIT, 1024], F32R)
        y_mix = sb("y_mix", [P, 8, T])
        ysa = y_mix[:, 0:4, :]
        yret = y_mix[:, 4:8, :]
        cst = sb("cst", [P, 5 * P])
        ident, ones, blk, rot_sa, rot_ret = (cst[:, P * i:P * i + P] for i in range(5))
        masks = sb("masks", [P, NMASK, C])
        small = sb("small", [P, 16])
        par = sb("par", [P, NPAR])
        region_a = sb("region_a", [P, 4 * TX + 4])
        n_root = sb("n_root", [P, T])
        WORDS_B = 21184
        with nc.sbuf_tensor("region_b", [P, WORDS_B], F32) as region_b:
            pass
        in_hi = sb("in_hi", [P, 12, T], F32R)
        in_lo = sb("in_lo", [P, 12, T], F32R)
        ra = region_a

        class Carve:
            def __init__(self):
                self.at = 0

            def __call__(self, *shape):
                n = int(np.prod(shape))
                assert self.at + n <= WORDS_B, (self.at, n)
                v = region_b[:, self.at:self.at + n]
                self.at += n
                if len(shape) == 2:
                    v = v.rearrange("p (a b) -> p a b", b=shape[1])
                if len(shape) == 3:
                    v = v.rearrange("p (a b c) -> p a b c", b=shape[1], c=shape[2])
                return v

        n_sq = ra[:, 0:2 * T].rearrange("p (a b) -> p a b", b=T)
        n_t = ra[:, 2 * T:4 * T].rearrange("p (a b) -> p a b", b=T)
        n_rs = n_root[:, :]
        cr = Carve()
        rq = ra[:, 0:4 * T].rearrange("p (a b) -> p a b", b=T)
        rk, rv, rg = cr(4, T), cr(4, T), cr(4, T)
        r_cos, r_sin = cr(T), cr(T)
        r_tab = region_b[:, cr.at - 2 * T:cr.at]
        t_raw, t_cos, t_rot = cr(2, T), cr(2, T), cr(2, T)
        r_dmask, r_gam, r_qdec, r_kdec = cr(4, P), cr(4, P), cr(4, P), cr(4)
        r_con = region_b[:, cr.at - 3 * 512 - 4:cr.at]
        k_st, v_st, q_st, q_dec, sc_sb, k_tm, v_tm = (cr(4, P) for _ in range(7))
        st0, st1, st_s, st_t = (cr(4, P) for _ in range(4))
        cw = Carve()
        a_kk = ra[:, 0:4 * TX].rearrange("p (a b) -> p a b", b=TX)
        a_r, a_k, a_v = (cw(4, TX) for _ in range(3))
        xwa, xg = cw(TX), cw(TX)
        pt = cw(2, TX + 1)
        d_t = cw(TX)
        shift_out = cw(28)
        gate_dsa = ra[:, 2 * T:4 * T].rearrange("p (a b) -> p a b", b=T)
        cs = Carve()
        cs.at = cw.at
        qi = ra[:, 0:2 * T].rearrange("p (a b) -> p a b", b=T)
        kd = cs(2, T + TP)
        ki = cs(T + TP)
        v_new, v_old = cs(5, P), cs(4, P)
        wi = cs(5, 4)
        k_rope, v_ch = cs(T), cs(T)
        top8 = cs(8)
        prob_t = cs(2, 512)
        stat = cs(2, 4)
        s_at = cs.at
        s_cos, s_sin = cs(T), cs(T)
        s_tab = region_b[:, cs.at - 2 * T:cs.at]
        s_raw, s_tcos, s_trot = cs(2, T), cs(2, T), cs(2, T)
        cs.at = s_at
        relu_sb = cs(2, T)
        score, bias = cs(T), cs(T)
        logit, prob = cs(2, T), cs(2, T)
        a_b = cw(4, TX)
        cum = cw(4, NC * 65)
        lora_g = cw(512)
        w_at = cw.at
        lora_wa = cw(512)
        lw, cmask = cw(2, NC * 65), cw(NC * 65)
        sq_t, clamped = pt[:, :, 0:TX], cw(4, TX)
        z_at = WORDS_B - 512
        assert cw.at <= z_at
        cw.at = w_at
        be, ka, LT, XX = (cw(512) for _ in range(4))
        M1, BTs = cw(512), [cw(512), cw(512)]
        R_sb, U_sb, z_t = (cw(256) for _ in range(3))
        w_ends = [cw(8), cw(8)]
        gate_out = cw(2, T)
        assert cw.at <= z_at
        cw.at = z_at
        Z0, Z1 = cw(256), cw(256)
        sets = [[t.rearrange("p a b -> p (a b)")[:, n * 512:(n + 1) * 512] for n in range(9)]
                for t in (y_mix[:, :, :], x[:, :, :])]
        cp = Carve()
        cp.at = w_at
        p_sq, p_rs, p_rk, p_bv, p_y = (cp(2, TX) for _ in range(5))
        gate_in = ysa[:, 0:3, :]
        merged = yret[:, 0:2, :]
        gated = yret[:, 2:4, :]
        relu_m = yret[:, 0:2, :]
        sq_m = yret[:, 2:4, :]

        dense = [ctx.enter_context(nc.psum_tensor(f"dense{i}", [P, 1024], F32)) for i in range(2)]
        mix = [ctx.enter_context(nc.psum_tensor(f"mix{i}", [P, 1024], F32)) for i in range(2)]
        r_ps, y_ps, z_ps = (dense[1][:, 256 * i:256 * i + 256] for i in range(3))
        u_ps = r_ps
        bank = [mix[0][:, 0:512], mix[0][:, 512:1024], mix[1][:, 0:512], mix[1][:, 512:1024]]

        gate_dram = nc.dram_tensor("gate_scratch", (N_GATE, P, T), F32, kind="Internal").ap()
        x_dram = nc.dram_tensor("x_scratch", (P, KT, T), F32, kind="Internal").ap()
        y_dram = nc.dram_tensor("y_scratch", (P, KT, T), F32, kind="Internal").ap()

        R5, C9 = 5, NC

        in_x, in_const, in_par = sem("in_x"), sem("in_const"), sem("in_par")
        in_ret, in_sa, in_rw, in_g2 = sem("in_ret"), sem("in_sa"), sem("in_rw"), sem("in_g2")
        gate_stored = [sem("gate_stored0"), sem("gate_stored1")]
        in_gate = [sem(f"in_gate{i}") for i in range(3)]
        x_away, y_away, x_back, y_back = sem("x_away"), sem("y_away"), sem("x_back"), sem("y_back")
        gate_ready, out_stored = sem("gate_ready"), sem("out_stored")
        w_loaded = [sem(f"w_loaded{i}") for i in range(RAW)]
        w_high, w_split, w_used = sem("w_high"), sem("w_split"), sem("w_used")
        dense_free = [sem("dense_free0"), sem("dense_free1")]
        sq_ready, ssq_ready, rs_ready, act_ready = sem("sq_ready"), sem("ssq_ready"), sem("rs_ready"), sem("act_ready")
        normed, high_ready = sem("normed"), sem("high_ready")
        rope_raw, rope_rot, rope_done = sem("rope_raw"), sem("rope_rot"), sem("rope_done")
        ret_sig = sem("ret_sig")
        ret_pe = Steps(sem("ret_pe"), R5, ["turned", "gram", "state"])
        ret_dve = Steps(sem("ret_dve"), R5, ["staged", "k_tm", "scores"])
        ret_act = Steps(sem("ret_act"), R5, ["v_tm", "out"])
        ret_cross, ret_state = sem("ret_cross"), sem("ret_state")
        post_act = Steps(sem("post_act"), 1, ["sq0", "sq1", "rs0", "sq2", "rs1", "sq3", "rs2", "rs3"])
        post_pe, post_dve = sem("post_pe"), sem("post_dve")
        sa_v, sa_pe, sa_act, sa_dve = sem("sa_v"), sem("sa_pe"), sem("sa_act"), sem("sa_dve")
        ix_pe, ix_act, ix_dve = sem("ix_pe"), sem("ix_act"), sem("ix_dve")
        at_scores, at_logits, at_exp, at_probs = sem("at_scores"), sem("at_logits"), sem("at_exp"), sem("at_probs")
        at_turned, at_values = sem("at_turned"), sem("at_values")
        at_turned_sb, at_out = sem("at_turned_sb"), sem("at_out")
        shift_act, shift_dve = sem("shift_act"), sem("shift_dve")
        lora_act = Steps(sem("lora_act"), 1, [f"{s}{j}" for s in ("sq", "sig", "norm") for j in range(4)])
        lora_pe = Steps(sem("lora_pe"), 1, [f"{s}{j}" for s in ("ssq", "lora") for j in range(4)])
        lora_dve = Steps(sem("lora_dve"), 1, [f"{s}{j}" for s in ("kk0_", "clamp", "scan", "kk") for j in range(4)])
        last = len(LEVELS) - 1
        lev = [(n, h) for n in range(last + 1) for h in (0, 1)]
        rw_pe = Steps(sem("rw_pe"), R5, ["gram", "turned"]
                      + [f"{k}_{n}_{h}" for n in range(last + 1) for k in ("m1", "x") for h in (0, 1)])
        rw_act = Steps(sem("rw_act"), R5, ["lt", "v_tm", "turned"] + [f"m1_{n}_{h}" for n, h in lev])
        rw_exp, rw_staged = sem("rw_exp"), sem("rw_staged")
        rw_dve = Steps(sem("rw_dve"), R5, ["gram", "tk", "b_0"]
                       + [f"{k}_{n + d}_{h}" for n in range(last) for h in (0, 1) for k, d in (("b", 1), ("x", 0))]
                       + [f"x_{last}_0", f"x_{last}_1"])
        ch_pe = Steps(sem("ch_pe"), C9, ["r", "u", "z", "y"])
        ch_act = Steps(sem("ch_act"), C9, ["r", "u", "y"])
        ch_z, lw_clear = sem("ch_z"), sem("lw_clear")
        both = lambda *names: [name + str(p) for name in names for p in (0, 1)]
        gn_pe = Steps(sem("gn_pe"), 2, both("mean", "var", "bonus", "gate"))
        gn_act = Steps(sem("gn_act"), 2, both("sq", "rs"))
        gn_dve = Steps(sem("gn_dve"), 2, both("yc", "rk", "out"))
        br_split, br_gated, mlp_act, mlp_split, fin = (
            sem("br_split"), sem("br_gated"), sem("mlp_act"), sem("mlp_split"), sem("fin"))

        waited_pe, waited_dve, waited_pool = sem("waited_pe"), sem("waited_dve"), sem("waited_pool")

        block = ctx.enter_context(nc.Block())
        OUTS = 8 * 16

        def pr(name, i):
            at = PARAMS[name][0] + i
            return par[:, at:at + 1]

        def out_of(ps):
            return ps.rearrange("p (a b) -> p a b", b=512)[:, :, 0:HALF]

        def halves(t):
            return t.rearrange("p (a b) -> p a b", b=HALF)

        def cum_view(lo, c0, nch):
            return cum.rearrange("p j (c t) -> p j c t", t=65)[:, :, bass.ds(c0, nch), lo:lo + C]

        def blocks3(t, n):
            return t[:, 0:n * C].rearrange("p (g t) -> p g t", t=C)

        def mask3(m, n):
            return masks[:, m, :].unsqueeze(1).broadcast_to([P, n, C])

        @block.sync
        def _(sp):
            sp.dma_start(x[:, :, :], dr["x"]).then_inc(in_x, 16)
            sp.dma_start(cst[:, :], dr["cst"]).then_inc(in_const, 16)
            sp.dma_start(masks[:, :, :], dr["masks"]).then_inc(in_const, 16)
            sp.dma_start(small[:, :], dr["small"]).then_inc(in_const, 16)
            for s in range(RAW):
                sp.dma_start(w_raw[:, s, :], dr["stream"][s]).then_inc(w_loaded[s], 16)
            with sp.Fori(1, DEPTH * NT // RAW) as g:
                for s in range(RAW):
                    sp.wait_ge(w_split, (g - 1) * RAW + s + 1)
                    sp.dma_start(w_raw[:, s, :],
                                 dr["stream"][bass.ds(g * RAW + s, 1), :, :].rearrange("a p n -> p (a n)")
                                 ).then_inc(w_loaded[s], 16)

        @block.gpsimd
        def _(pool):
            def split(g, s, used):
                v = s % SPLIT
                pool.wait_ge(w_loaded[s], g * 16 + 16)
                if used is not None:
                    pool.wait_ge(w_used, used)
                if used is not None:
                    pool.sem_inc(waited_pool, 1)
                nc.gpsimd.tensor_scalar(w_hi[:, v, :], w_raw[:, s, :], 1.0, 1.0, ALU.mult,
                                        ALU.mult).then_inc(w_high, 1)
                pool.wait_ge(w_high, g * RAW + s + 1)
                nc.gpsimd.tensor_tensor(w_lo[:, v, :], w_raw[:, s, :], w_hi[:, v, :].bitcast(F32),
                                        ALU.subtract).then_inc(w_split, 1)

            for s in range(RAW):
                split(0, s, 2 * (s - SPLIT + 1) if s >= SPLIT else None)
            with pool.Fori(1, DEPTH * NT // RAW) as g:
                for s in range(RAW):
                    split(g, s, g * (2 * RAW) + 2 * (s - SPLIT + 1))

        @block.tensor
        def _(pe):
            def acc(out, lhsT, rhs, start, stop):
                return nc.tensor.matmul(out, lhsT, rhs, start=start, stop=stop, skip_group_check=True)

            def wide(out, lhsT, rhs, width, start=True, stop=True):
                acc(out[:, 0:512], lhsT, rhs[:, 0:512], start, stop)
                return acc(out[:, 512:width], lhsT, rhs[:, 512:width], start, stop)

            def dense_slice(buf, slot, hi, lo, w_k, x_k, first, stop):
                wh, wl = (w[:, slot, w_k * P:w_k * P + P] for w in (w_hi, w_lo))
                parts = [(slice(512 * i, 512 * i + HALF), slice(HALF * i, HALF * i + HALF)) for i in range(2)]
                for out, tok in parts:
                    acc(buf[:, out], wh, hi[:, x_k, tok], first, False)
                    acc(buf[:, out], wh, lo[:, x_k, tok], False, False)
                for out, tok in parts:
                    mm = acc(buf[:, out], wl, hi[:, x_k, tok], False, stop)
                return mm

            def dense_tile(slot, buffer, split_count, free_count, hi, lo, k0=0, ks=KT, half=0, fresh=None, used=2):
                buf = dense[buffer]
                pe.wait_ge(w_split, split_count)
                pe.wait_ge(dense_free[buffer], free_count)
                for k in range(ks):
                    if fresh:
                        fresh(k)
                    mm = dense_slice(buf, slot, hi, lo, half * ks + k, k0 + k, k == 0, k == ks - 1)
                mm.then_inc(w_used, used)

            def tile(l, t, u, hi, lo, **kw):
                dense_tile(t % SPLIT, u % 2, l * NT + t + 1, free_before(u, l), hi, lo,
                           used=1 if kw.get("ks") == 4 else 2, **kw)

            def fill(l, t0, slices):
                for s in range(*slices):
                    t, k = t0 + s // KT, s % KT
                    buffer = buffer_of(t)
                    if k == 0:
                        pe.wait_ge(w_split, l * NT + (t + 1))
                        pe.wait_ge(dense_free[buffer], free_before(t, l))
                    mm = dense_slice(dense[buffer], t % SPLIT, act_hi, act_lo, k, k, k == 0, k == KT - 1)
                    if k == KT - 1:
                        mm.then_inc(w_used, 4 if t == T_SPARE - 1 else 2)

            def sum_squares(n):
                for k in range(KT):
                    pe.wait_ge(sq_ready, n * KT + k + 1)
                    wide(mix[0], ones, n_sq[:, k % 2, :], T, k == 0, k == KT - 1).then_inc(ssq_ready, 1)

            def rotate(l, n, mat, src):
                pe.wait_ge(rope_raw, l * 16 + (n + 1))
                if n >= 2:
                    pe.wait_ge(rope_done, l * 16 + (n - 1))
                wide(mix[n % 2], mat, src[:, n % 2, :], T).then_inc(rope_rot, 1)

            def retention_step(l, i, n, s_in, s_mid):
                ch = l * C9 + 2 * i
                chunks = n // C
                first = 4 * i

                def early(n):
                    nonlocal first
                    if i < 4:
                        fill(l, T_SA, (first, first + n))
                        first += n

                pe.wait_ge(ret_dve.sem, ret_dve.at("staged", l, i))
                passed()
                for h in range(4):
                    nc.tensor.transpose(bank[0][0:n, h * P:(h + 1) * P], k_st[:, h, 0:n], ident)
                for h in range(4):
                    mm = nc.tensor.transpose(bank[1][0:n, h * P:(h + 1) * P], v_st[:, h, 0:n], ident)
                mm.then_inc(ret_pe.sem, 1)
                for h in range(4):
                    mm = acc(bank[2][0:n, h * P:h * P + n], k_st[:, h, 0:n], q_st[:, h, 0:n], True, True)
                mm.then_inc(ret_pe.sem, 1)
                early(2)
                pe.wait_ge(ret_dve.sem, ret_dve.at("k_tm", l, i))
                pe.wait_ge(ret_act.sem, ret_act.at("v_tm", l, i))
                passed()
                for q in range(chunks):
                    for h in range(4):
                        mm = acc(bank[q][:, h * P:(h + 1) * P], k_tm[q * C:(q + 1) * C, h, :],
                                 v_tm[q * C:(q + 1) * C, h, :], True, True)
                mm.then_inc(ret_pe.sem, 1)
                early(1)
                pe.wait_ge(ret_dve.sem, ret_dve.at("scores", l, i))
                passed()
                for h in range(4):
                    acc(bank[3][:, h * P:h * P + n], v_tm[0:n, h, :], sc_sb[0:n, h, 0:n], h == 0, False)
                for h in range(4):
                    mm = acc(bank[3][:, h * P:h * P + C], s_in[:, h, :], q_dec[:, h, 0:C], False, chunks == 1)
                mm.then_inc(ret_cross, 1)
                if chunks == 2:
                    early(1)
                    pe.wait_ge(ret_state, ch + 1)
                    passed()
                    for h in range(4):
                        mm = acc(bank[3][:, h * P + C:h * P + 2 * C], s_mid[:, h, :], q_dec[:, h, C:2 * C], False, True)
                    mm.then_inc(ret_cross, 1)

            def rwkv_body(l, body, f, s):
                rows2 = [slice(0, C), slice(C, P)]

                def per_block(out, lhsT, rhs, blocks=None, at=0):
                    blocks = blocks or range(4 * STEP_CHUNKS[f])
                    for n, g in enumerate(blocks):
                        for rows in rows2:
                            b = slice(g * C, g * C + C)
                            mm = acc(out[rows, at + n * C:at + n * C + C], lhsT[rows, b], rhs[rows, b], True, True)
                    return mm

                if f is not None:
                    
                    al, rh, LkT, TbT, TkT, Vt, kat, bet, XT = sets[f % 2]

                    def gram():
                        pe.wait_ge(rw_staged, l * R5 + (f + 1))
                        if f:
                            pe.wait_ge(rw_dve.sem, rw_dve.at(f"x_{last}_1", l, f - 1))
                        passed()
                        per_block(bank[0], be, al)
                        per_block(bank[1], al, be)
                        per_block(bank[2], ka, al)
                        per_block(bank[3], be, rh).then_inc(rw_pe.sem, 1)

                    def turn():
                        pe.wait_ge(rw_dve.sem, rw_dve.at("gram", l, f))
                        pe.wait_ge(rw_act.sem, rw_act.at("lt", l, f))
                        passed()
                        for src, dst in ((TkT, bank[1]), (ka, bank[2]), (be, bank[3])):
                            for g in range(4 * STEP_CHUNKS[f]):
                                for rows in rows2:
                                    b = slice(g * C, g * C + C)
                                    acc(dst[rows, b], src[rows, b], masks[rows, M_EYE, :], True, True)
                        per_block(bank[0], ka, rh).then_inc(rw_pe.sem, 1)

                    halves2 = [range(h * 2 * STEP_CHUNKS[f], (h + 1) * 2 * STEP_CHUNKS[f]) for h in (0, 1)]

                    def level_m1(n):
                        for h in (0, 1):
                            if n == 0:
                                pe.wait_ge(rw_act.sem, rw_act.at("turned", l, f))
                                pe.wait_ge(rw_dve.sem, rw_dve.at("b_0", l, f))
                            else:
                                pe.wait_ge(rw_dve.sem, rw_dve.at(f"b_{n}_{h}", l, f))
                            passed()
                            per_block(bank[3 * h], BTs[n % 2], XX, halves2[h]).then_inc(rw_pe.sem, 1)

                    def level_x(n):
                        for h in (0, 1):
                            pe.wait_ge(rw_act.sem, rw_act.at(f"m1_{n}_{h}", l, f))
                            if n:
                                pe.wait_ge(rw_dve.sem, rw_dve.at(f"x_{n - 1}_{h}", l, f))
                            passed()
                            if n < last:
                                per_block(bank[1 + h], XT, M1, halves2[h])
                            per_block(bank[1 + h], M1, XT, halves2[h], 256).then_inc(rw_pe.sem, 1)

                if s is not None:
                    nq = STEP_CHUNKS[s]
                    Z = (Z0, Z1)[s == R5 - 1]
                    al_, rh_, LkT_, TbT_, TkT_, Vt_, kat_, bet_, XT_ = sets[s % 2]
                    if f is None:
                        pe.wait_ge(rw_dve.sem, rw_dve.at(f"x_{last}_1", l, s))
                        passed()

                    def blocks(q):
                        return [(rows, slice((j * nq + q) * C, (j * nq + q + 1) * C), slice(j * C, (j + 1) * C))
                                for j in range(4) for rows in rows2]

                    def chunk_r(q):
                        if s or q:
                            pe.wait_ge(ch_act.sem, ch_act.at("y", l, 2 * s + q - 1))
                        pe.wait_ge(ch_z, l * C9 + (START + 2 * s + q))
                        passed()
                        for rows, g, o in blocks(q):
                            acc(r_ps[rows, o], al_[rows, g], Z[rows, o], True, False)
                            mm = acc(r_ps[rows, o], LkT_[rows, g], Vt_[rows, g], False, True)
                        mm.then_inc(ch_pe.sem, 1)

                    def chunk_u(q):
                        pe.wait_ge(ch_act.sem, ch_act.at("r", l, 2 * s + q))
                        passed()
                        for rows, g, o in blocks(q):
                            mm = acc(u_ps[rows, o], XT_[rows, g], R_sb[rows, o], True, True)
                        mm.then_inc(ch_pe.sem, 1)

                    def chunk_yz(q):
                        pe.wait_ge(ch_act.sem, ch_act.at("u", l, 2 * s + q))
                        passed()
                        for rows, g, o in blocks(q):
                            acc(z_ps[rows, o], kat_[rows, g], Vt_[rows, g], True, False)
                            mm = acc(z_ps[rows, o], bet_[rows, g], U_sb[rows, o], False, True)
                        mm.then_inc(ch_pe.sem, 1)
                        for rows, g, o in blocks(q):
                            acc(y_ps[rows, o], Z[rows, o], rh_[rows, g], True, False)
                            acc(y_ps[rows, o], U_sb[rows, o], TbT_[rows, g], False, False)
                            mm = acc(y_ps[rows, o], Vt_[rows, g], TkT_[rows, g], False, True)
                        mm.then_inc(ch_pe.sem, 1)

                def beside(stage):
                    fill(l, T_GATE_RW, body_range(body, stage))

                if s is None:
                    gram()
                    beside(0)
                    turn()
                    beside(1)
                    for n in range(last + 1):
                        level_m1(n)
                        beside(2 + 2 * n)
                        level_x(n)
                        beside(3 + 2 * n)
                elif f is None:
                    chunk_r(0)
                    beside(0)
                    chunk_u(0)
                    beside(1)
                    chunk_yz(0)
                    beside(2)
                else:
                    gram()
                    beside(0)
                    chunk_r(0)
                    beside(1)
                    turn()
                    beside(2)
                    chunk_u(0)
                    beside(3)
                    level_m1(0)
                    beside(4)
                    chunk_yz(0)
                    beside(5)
                    level_x(0)
                    beside(6)
                    level_m1(1)
                    beside(7)
                    chunk_r(1)
                    beside(8)
                    level_x(1)
                    beside(9)
                    chunk_u(1)
                    beside(10)
                    level_m1(2)
                    beside(11)
                    chunk_yz(1)
                    beside(12)
                    level_x(2)
                    beside(13)
                    for n in range(3, last + 1):
                        level_m1(n)
                        beside(8 + 2 * n)
                        level_x(n)
                        beside(9 + 2 * n)

            def passed():
                pe.sem_inc(waited_pe, 1)

            pe.wait_ge(in_const, 48)
            sum_squares(0)
            with pe.Fori(0, DEPTH) as l:
                for t in range(N_RET):
                    fresh = (lambda k: pe.wait_ge(act_ready, l * (2 * KT) + k + 1)) if t == 0 else None
                    tile(l, T_RET + t, T_RET + t, act_hi, act_lo, fresh=fresh)
                    if 1 <= t <= 8:
                        rotate(l, t - 1, rot_ret, t_raw)
                for i in range(4):
                    retention_step(l, i, P, st0, st1)
                retention_step(l, 4, C, st_s, None)
                pe.wait_ge(ret_state, l * C9 + C9)
                for h in range(4):
                    pe.wait_ge(post_act.sem, post_act.at(f"sq{h}", l))
                    wide(mix[h % 2], ones, t_raw[:, h % 2, :], T).then_inc(post_pe, 1)

                rotary = {0: 8, 1: 9, 2: 10, 3: 11, 4: 12, 6: 13, 7: 14, 8: 15}
                for t in range(N_SA):
                    if t >= 2:
                        tile(l, T_SA + t, T_SA + t, act_hi, act_lo)
                    if t == 0:
                        pe.wait_ge(post_dve, l * 4 + 4)
                    if t - 1 in rotary:
                        rotate(l, rotary[t - 1], rot_sa, s_raw)
                rotate(l, 15, rot_sa, s_raw)
                pe.wait_ge(sa_v, l + 1)
                pe.wait_ge(rope_done, l * 16 + 16)
                passed()
                for src, at in ((v_ch, 0), (s_raw[:, 1, :], 2)):
                    for b in range(5):
                        n = P if b < 4 else C
                        out = bank[at][0:n, b * P:(b + 1) * P] if b < 4 else bank[at + 1][0:n, 0:P]
                        mm = nc.tensor.transpose(out, src[:, b * P:b * P + n], ident)
                mm.then_inc(sa_pe, 1)

                pe.wait_ge(sa_dve, l + 1)
                pe.wait_ge(sa_act, l + 1)
                pe.wait_ge(in_sa, l * 128 + 128)
                for b in range(5):
                    n, t0 = (P if b < 4 else C), b * P
                    keys = (b + 1) * P if b < 4 else T
                    nb = (keys + P - 1) // P

                    def against(out, lhsT, keys_t, half):
                        rows = slice(half * C, half * C + C)
                        if b < 4:
                            return acc(out[0:n, 0:keys], lhsT, keys_t[rows, 0:keys], True, True)
                        acc(out[0:n, 0:512], lhsT, keys_t[rows, T:T + TP], True, True)
                        return acc(out[0:n, 512:T], lhsT, keys_t[rows, TP:T], True, True)

                    if b:
                        pe.wait_ge(at_out, l * 40 + (b * 8))
                        passed()
                        for i in range(4):
                            if i >= 2:
                                pe.wait_ge(ix_act, l * 16 + (b - 1) * 4 + i - 1)
                                passed()
                            half = i % 2
                            against(mix[half], qi[half * C:half * C + C, i // 2, t0:t0 + n], ki, half).then_inc(ix_pe, 1)
                        fill(l, T_RW, fill_range(b))
                        pe.wait_ge(ix_act, l * 16 + b * 4)
                        passed()

                    def scores(h):
                        half, run = h % 2, b * 8 + h
                        if h >= 2:
                            pe.wait_ge(at_out, l * 40 + (run - 1))
                            passed()
                        against(mix[half], ysa[half * C:half * C + C, h // 2, t0:t0 + n],
                                kd[:, h // 4, :], half).then_inc(at_scores, 1)

                    scores(0)
                    for h in range(8):
                        half, run = h % 2, b * 8 + h
                        if h < 7:
                            scores(h + 1)
                        fill(l, T_RW, fill_range(b, h, 0))
                        pe.wait_ge(at_probs, l * 40 + (run + 1))
                        passed()
                        for kb in range(nb):
                            w = min(P, keys - kb * P)
                            mm = nc.tensor.transpose(mix[half][0:w, kb * n:(kb + 1) * n],
                                                     prob[0:n, half, kb * P:kb * P + w], ident[0:n, 0:n])
                        mm.then_inc(at_turned, 1)
                        fill(l, T_RW, fill_range(b, h, 1))
                        pe.wait_ge(at_turned_sb, l * 40 + (run + 1))
                        passed()
                        for kb in range(nb):
                            w = min(P, keys - kb * P)
                            vv = v_new[:, kb, :] if b < 4 else v_old[:, kb, :] if kb < 4 else v_new[:, 4, :]
                            mm = acc(mix[half][half * C:half * C + C, 768:768 + n],
                                     vv[0:w, (h // 4) * C:(h // 4) * C + C],
                                     prob_t[0:w, half, kb * n:(kb + 1) * n], kb == 0, kb == nb - 1)
                        mm.then_inc(at_values, 1)

                pe.wait_ge(dense_free[0], free_before(T_GATE_RW, l))
                pe.wait_ge(dense_free[1], free_before(U_BR + 1, l))
                passed()
                for j in range(4):
                    pe.wait_ge(lora_act.sem, lora_act.at(f"sq{j}", l))
                    if j >= 2:
                        pe.wait_ge(lora_dve.sem, lora_dve.at(f"clamp{j - 2}", l))
                    wide(dense[j % 2], blk, sq_t[:, j % 2, :], TX).then_inc(lora_pe.sem, 1)
                pe.wait_ge(in_rw, l * 48 + 48)
                for j in range(4):
                    w_ps, a_ps = (mix, dense)[j % 2]
                    if j < 2:
                        pe.wait_ge(lora_dve.sem, lora_dve.at("clamp3", l))
                    else:
                        pe.wait_ge(lora_act.sem, lora_act.at(f"sig{j - 2}", l))
                    passed()
                    wide(w_ps, lora_wa[0:C, j * P:(j + 1) * P], xwa[0:C, :], TX)
                    wide(a_ps, lora_wa[C:P, j * P:(j + 1) * P], xwa[C:P, :], TX).then_inc(lora_pe.sem, 1)
                for body, (f, s) in enumerate(RW_BODIES):
                    rwkv_body(l, body, f, s)

                pe.wait_ge(in_g2, l * 16 + 16)
                pe.wait_ge(ch_z, l * C9 + (START + C9))
                pe.wait_ge(ch_act.sem, ch_act.at("y", l, C9 - 1))
                pe.wait_ge(dense_free[0], free_before(U_BR, l))
                for g in range(2):
                    sums = [(p, 2 * g + p, (mix, dense)[p]) for p in (0, 1)]
                    for p, j, ps in sums:
                        if g:
                            pe.wait_ge(gn_dve.sem, gn_dve.at(f"out{p}", l, g - 1))
                        wide(ps[0], blk, a_kk[:, j, :], TX).then_inc(gn_pe.sem, 1)
                    for p, j, ps in sums:
                        pe.wait_ge(gn_act.sem, gn_act.at(f"sq{p}", l, g))
                        wide(ps[1], blk, p_sq[:, p, :], TX).then_inc(gn_pe.sem, 1)
                    for p, j, ps in sums:
                        pe.wait_ge(gn_dve.sem, gn_dve.at(f"rk{p}", l, g))
                        wide(ps[0], blk, p_rk[:, p, :], TX).then_inc(gn_pe.sem, 1)
                    for p, j, ps in sums:
                        pe.wait_ge(gn_act.sem, gn_act.at(f"rs{p}", l, g))
                        wide(ps[1], lora_g[:, j * P:(j + 1) * P], xg, TX).then_inc(gn_pe.sem, 1)
                pe.wait_ge(gn_dve.sem, gn_dve.at("out1", l, 1))

                for mp in range(4):
                    for b in range(3):
                        for mi in range(2):
                            n = (mp * 3 + b) * 2 + mi
                            fresh = (lambda k, b=b: pe.wait_ge(br_split, l * 12 + b * 4 + k + 1)) \
                                if mp == 0 and mi == 0 else None
                            tile(l, T_BR + mp * 3 + b, U_BR + n, in_hi, in_lo, k0=b * 4, ks=4, half=mi, fresh=fresh)
                for m in range(KT):
                    fresh = (lambda k: pe.wait_ge(br_gated, l * KT + k + 1)) if m == 0 else None
                    tile(l, T_WO + m, U_WO + m, act_hi, act_lo, fresh=fresh)
                sum_squares(l * 2 + 1)
                with pe.Fori(0, FF) as c:
                    for m in range(2 * KT):
                        up = m < KT
                        fresh = None
                        if m == 0:
                            fresh = lambda k: pe.wait_ge(act_ready, l * (2 * KT) + (KT + k + 1))
                        if m == KT:
                            fresh = lambda k: pe.wait_ge(mlp_split, START + l * (FF * KT) + c * KT + k + 1)
                        dense_tile(m % SPLIT, m % 2, l * NT + T_MLP + c * (2 * KT) + m + 1,
                                   free_before(U_MLP + m, l) + c * KT,
                                   act_hi if up else in_hi, act_lo if up else in_lo, fresh=fresh)
                sum_squares(l * 2 + 2)

        @block.scalar
        def _(act):
            def op(out, in_, func, **kw):
                return nc.scalar.activation(out, in_, func, **kw)

            def taken(l, u, t, half=0):
                act.wait_ge(w_used, used_after(t, l, half))
                return out_of(dense[buffer_of(u)])

            def squares(n, waits):
                nc.scalar.preload_act_table_set(EXP_LN)
                for k in range(KT):
                    waits(k)
                    if k >= 2:
                        act.wait_ge(ssq_ready, n * KT + k - 1)
                    op(n_sq[:, k % 2, :], x[:, k, :], ACT.Square).then_inc(sq_ready, 1)

            def root(out, ps, width, scale, eps_col):
                op(out, ps[:, 0:width], ACT.Ln, scale=scale, bias=small[:, eps_col:eps_col + 1])
                nc.scalar.drain()
                return op(out, out, ACT.Exp, scale=-0.5)

            def norm_root(n):
                act.wait_ge(ssq_ready, n * KT + KT)
                root(n_rs, mix[0], T, 1.0 / D, 0).then_inc(rs_ready, 1)

            def high_parts(l, which):
                for k in range(KT):
                    act.wait_ge(normed, l * (2 * KT) + (which * KT + k + 1))
                    op(act_hi[:, k, :], n_t[:, k % 2, :], ACT.Copy).then_inc(high_ready, 1)

            def after_dve(l, u0):
                return lambda k: act.wait_ge(dense_free[(u0 + k) % 2], free_before(u0 + k, l, 1))

            def retention_step(l, i, n):
                ch = l * C9 + 2 * i
                act.wait_ge(ret_pe.sem, ret_pe.at("turned", l, i))
                op(v_tm[0:n], bank[1][0:n, :].rearrange("p (h e) -> p h e", e=P), ACT.Copy).then_inc(ret_act.sem, 1)
                act.wait_ge(ret_cross, START + ch + n // C)
                op(yret[:, :, bass.ds(i * P, n)], bank[3][:, :].rearrange("p (h t) -> p h t", t=P)[:, :, 0:n],
                   ACT.Copy).then_inc(ret_act.sem, 1)

            def gates_away(l, t0, tiles, gate_out):
                for n in tiles:
                    u, t = t0 + n, t0 + n - T_GATE
                    buf = taken(l, u, u)
                    if t >= 2:
                        act.wait_ge(gate_stored[t % 2], l * (16 * N_GATE // 2) + 16 * (t // 2))
                    op(halves(gate_out[:, t % 2, :]), buf, ACT.Copy).then_inc(dense_free[buffer_of(u)], 1)
                    act.wait_ge(dense_free[buffer_of(u)], free_before(u, l, 1))
                    act.dma_start(gate_dram[t], gate_out[:, t % 2, :]).then_inc(gate_stored[t % 2], 16)

            def rwkv_stage(l, f):
                nq, (al, rh, *_) = STEP_CHUNKS[f], sets[f % 2]
                view = lambda t: t[:, 0:4 * nq * C].rearrange("p (j c t) -> p j c t", j=4, t=C)
                act.wait_ge((y_away, x_away)[f % 2], l * 16 + 16)
                if f >= 1:
                    act.wait_ge(rw_pe.sem, rw_pe.at("turned", l, f - 1))
                if f >= 2:
                    act.wait_ge(ch_z, l * C9 + (START + 2 * (f - 1)))
                op(view(ka), cum_view(1, 2 * f, nq), ACT.Exp, scale=DECAY)
                op(view(al), cum_view(0, 2 * f, nq), ACT.Exp, scale=-DECAY)
                op(view(rh), cum_view(1, 2 * f, nq), ACT.Exp, scale=-DECAY).then_inc(rw_exp, 1)

            def rwkv_body(l, body, f, s):
                if f is not None:
                    w = 4 * STEP_CHUNKS[f] * C
                    al, rh, LkT, TbT, TkT, Vt, kat, bet, XT = sets[f % 2]

                    def gram():
                        act.wait_ge(rw_pe.sem, rw_pe.at("gram", l, f))
                        op(LT[:, 0:w], bank[0][:, 0:w], ACT.Copy).then_inc(rw_act.sem, 1)

                    def turn():
                        act.wait_ge(rw_pe.sem, rw_pe.at("turned", l, f))
                        op(Vt[:, 0:w], bank[1][:, 0:w], ACT.Copy).then_inc(rw_act.sem, 1)
                        op(kat[:, 0:w], bank[2][:, 0:w], ACT.Copy)
                        op(bet[:, 0:w], bank[3][:, 0:w], ACT.Copy).then_inc(rw_act.sem, 1)

                    def level(n):
                        for h in (0, 1):
                            b = slice(h * w // 2, (h + 1) * w // 2)
                            act.wait_ge(rw_pe.sem, rw_pe.at(f"m1_{n}_{h}", l, f))
                            op(M1[:, b], bank[3 * h][:, 0:w // 2], ACT.Copy).then_inc(rw_act.sem, 1)
                        if n == last - 1 and f + 1 < R5:
                            rwkv_stage(l, f + 1)

                if s is not None:
                    def chunk_r(q):
                        act.wait_ge(ch_pe.sem, ch_pe.at("r", l, 2 * s + q))
                        op(R_sb, r_ps, ACT.Copy).then_inc(ch_act.sem, 1)

                    def chunk_u(q):
                        act.wait_ge(ch_pe.sem, ch_pe.at("u", l, 2 * s + q))
                        op(U_sb, u_ps, ACT.Copy, scale=-1.0).then_inc(ch_act.sem, 1)

                    def chunk_y(q):
                        act.wait_ge(ch_pe.sem, ch_pe.at("y", l, 2 * s + q))
                        t0 = s * P + q * C if s < R5 - 1 else SX
                        op(a_kk[:, :, t0:t0 + C], y_ps.rearrange("p (j t) -> p j t", t=C),
                           ACT.Copy).then_inc(ch_act.sem, 1)

                def beside(stage):
                    gates_away(l, T_GATE_RW, done(*body_range(body, stage)), gate_out)

                if s is None:
                    gram()
                    beside(0)
                    turn()
                    beside(1)
                    for n in range(last + 1):
                        level(n)
                        beside(2 + 2 * n)
                        beside(3 + 2 * n)
                elif f is None:
                    chunk_r(0)
                    beside(0)
                    chunk_u(0)
                    beside(1)
                    chunk_y(0)
                    beside(2)
                else:
                    gram()
                    beside(0)
                    chunk_r(0)
                    beside(1)
                    turn()
                    beside(2)
                    chunk_u(0)
                    beside(3)
                    level(0)
                    beside(4)
                    chunk_y(0)
                    beside(5)
                    beside(6)
                    level(1)
                    beside(7)
                    chunk_r(1)
                    beside(8)
                    beside(9)
                    chunk_u(1)
                    beside(10)
                    level(2)
                    beside(11)
                    chunk_y(1)
                    beside(12)
                    beside(13)
                    for n in range(3, last + 1):
                        level(n)
                        beside(8 + 2 * n)
                        beside(9 + 2 * n)

            for s in (*dense_free, ret_cross, ch_z, mlp_split):
                act.sem_inc(s, START)
            act.wait_ge(in_x, 16)
            squares(0, lambda k: None)
            with act.Fori(0, DEPTH) as l:
                act.dma_start(par[:, :], layer_of(dr["par"], l)).then_inc(in_par, 16)
                act.dma_start(x_dram, x[:, :, :]).then_inc(x_away, 16)
                act.dma_start(r_tab, dr["r_tab"]).then_inc(in_ret, 16)
                act.dma_start(r_con, dr["r_con"]).then_inc(in_ret, 16)
                act.dma_start(st_s[:, :, :], layer_of(dr["st_ret"], l).rearrange("p (h e) -> p h e", e=P)).then_inc(in_ret, 16)
                act.wait_ge(in_const, 48)
                norm_root(l * 2)
                high_parts(l, 0)
                for t in range(N_RET):
                    if t < 8 and t >= 2:
                        act.wait_ge(rope_done, l * 16 + (t - 1))
                    buf = taken(l, T_RET + t, T_RET + t)
                    free = dense_free[t % 2]
                    if t < 8:
                        op(halves(t_raw[:, t % 2, :]), buf, ACT.Copy, scale=1.0 if t < 4 else RET_SCALE).then_inc(rope_raw, 1)
                        act.wait_ge(rope_raw, l * 16 + (t + 1))
                        act.sem_inc(free, 1)
                    elif t < 12:
                        op(halves(rv[:, t - 8, :]), buf, ACT.Copy).then_inc(free, 1)
                    else:
                        op(halves(rg[:, t - 12, :]), buf, ACT.Sigmoid).then_inc(ret_sig, 1)
                with act.Fori(0, 4) as i:
                    retention_step(l, i, P)
                act.wait_ge(ret_state, l * C9 + 8)
                act.dma_start(layer_of(outs["st_ret_p"], l).rearrange("p (h e) -> p h e", e=P), st0[:, :, :]).then_inc(out_stored, 16)
                retention_step(l, 4, C)
                nc.scalar.drain()
                act.wait_ge(ret_state, l * C9 + 9)
                act.dma_start(layer_of(outs["st_ret_s"], l).rearrange("p (h e) -> p h e", e=P), st1[:, :, :]).then_inc(out_stored, 16)
                nc.scalar.preload_act_table_set(EXP_LN)

                def post_sq(h):
                    if h >= 2:
                        act.wait_ge(post_pe, l * 4 + (h - 1))
                    op(t_raw[:, h % 2, :], yret[:, h, :], ACT.Square).then_inc(post_act.sem, 1)

                def post_rs(h):
                    act.wait_ge(post_pe, l * 4 + (h + 1))
                    if h >= 2:
                        act.wait_ge(post_dve, l * 4 + (h - 1))
                    root(t_cos[:, h % 2, :], mix[h % 2], T, 1.0 / P, 0).then_inc(post_act.sem, 1)

                for name in post_act.names:
                    (post_sq if name.startswith("sq") else post_rs)(int(name[-1]))

                act.wait_ge(post_dve, l * 4 + 4)
                act.wait_ge(out_stored, l * OUTS + 32)
                act.dma_start(s_tab, dr["s_tab"]).then_inc(in_sa, 16)
                for kv in range(2):
                    for half in range(2):
                        act.dma_start(kd[half * C:half * C + C, kv, T:T + TP],
                                      layer_of(dr["k_old"], l)[kv * C:kv * C + C, :]).then_inc(in_sa, 16)
                for half in range(2):
                    act.dma_start(ki[half * C:half * C + C, T:T + TP], layer_of(dr["ik_old"], l)).then_inc(in_sa, 16)
                act.dma_start(v_old[:, :, :], layer_of(dr["v_old"], l).rearrange("p (b e) -> p b e", e=P)).then_inc(in_sa, 16)
                rotary = {0: 8, 1: 9, 2: 10, 3: 11, 4: 12, 6: 13, 7: 14, 8: 15}
                for t in range(N_SA):
                    u = T_SA + t
                    n = rotary.get(t)
                    if n is not None:
                        act.wait_ge(rope_done, l * 16 + (n - 1))
                    buf = taken(l, u, u)
                    if n is not None:
                        op(halves(s_raw[:, n % 2, :]), buf, ACT.Copy).then_inc(rope_raw, 1)
                        act.wait_ge(rope_raw, l * 16 + (n + 1))
                    else:
                        op(halves(v_ch), buf, ACT.Copy).then_inc(sa_v, 1)
                        act.wait_ge(sa_v, l + 1)
                        act.dma_start(layer_of(outs["v_new"], l), v_ch).then_inc(out_stored, 16)
                    act.sem_inc(dense_free[u % 2], 1)
                act.wait_ge(rope_done, l * 16 + 16)
                act.dma_start(layer_of(outs["k_new"], l), k_rope).then_inc(out_stored, 16)
                act.dma_start(layer_of(outs["ik_new"], l), ki[0:C, 0:T]).then_inc(out_stored, 16)
                act.wait_ge(sa_pe, l + 1)
                op(v_new[:, 0:4, :], bank[0].rearrange("p (b e) -> p b e", e=P), ACT.Copy)
                op(v_new[0:C, 4, :], bank[1][0:C, 0:P], ACT.Copy).then_inc(sa_act, 1)
                nc.scalar.preload_act_table_set(EXP_LN)

                def filled(tiles):
                    for f in tiles:
                        if f >= N_RW:
                            gates_away(l, T_RW, [f], gate_dsa)
                            continue
                        u = T_RW + f
                        buf = taken(l, u, u)
                        if f >= 2:
                            act.wait_ge(shift_dve, l * N_RW + (f - 1))
                        op(pt[:, f % 2, 1:HALF + 1], buf[:, 0, :], ACT.Copy)
                        op(pt[:, f % 2, HALF + 1:TP + 1], buf[:, 1, 0:TP - HALF], ACT.Copy)
                        op(pt[:, f % 2, TP + 1:TP + 2], pr("shift", f), ACT.Copy)
                        op(pt[:, f % 2, TP + 2:TX + 1], buf[:, 1, TP - HALF:HALF], ACT.Copy).then_inc(shift_act, 1)
                        act.wait_ge(shift_act, l * N_RW + (f + 1))
                        act.sem_inc(dense_free[u % 2], 1)

                for b in range(5):
                    n, t0 = (P if b < 4 else C), b * P
                    keys = (b + 1) * P if b < 4 else T
                    nb = (keys + P - 1) // P
                    if b:
                        for i in range(4):
                            at = l * 16 + (b - 1) * 4 + i
                            act.wait_ge(ix_pe, at + 1)
                            if i >= 2:
                                act.wait_ge(ix_dve, at - 1)
                            op(relu_sb[0:n, i % 2, 0:keys], mix[i % 2][0:n, 0:keys], ACT.Relu,
                               scale=IDX_SCALE).then_inc(ix_act, 1)

                    def exps(h):
                        half, run = h % 2, b * 8 + h
                        act.wait_ge(at_logits, l * 40 + (run + 1))
                        if h >= 2:
                            act.wait_ge(at_turned, l * 40 + (run - 1))
                        op(prob[0:n, half, 0:keys], logit[0:n, half, 0:keys], ACT.Exp,
                           bias=stat[0:n, half, 1:2], accum_out=stat[0:n, half, 2:3]).then_inc(at_exp, 1)

                    filled(done(*fill_range(b)))
                    exps(0)
                    for h in range(8):
                        half, run = h % 2, b * 8 + h
                        filled(done(*fill_range(b, h, 0)))
                        act.wait_ge(at_turned, l * 40 + (run + 1))
                        if b < 4:
                            op(prob_t[:, half, 0:nb * n], mix[half][:, 0:nb * n], ACT.Copy).then_inc(at_turned_sb, 1)
                        else:
                            op(prob_t[:, half, 0:4 * n], mix[half][:, 0:4 * n], ACT.Copy)
                            op(prob_t[0:C, half, 4 * n:5 * n], mix[half][0:C, 4 * n:5 * n], ACT.Copy).then_inc(at_turned_sb, 1)
                        if h < 7:
                            exps(h + 1)
                        filled(done(*fill_range(b, h, 1)))
                        act.wait_ge(at_values, l * 40 + (run + 1))
                        rows = slice(half * C, half * C + C)
                        op(ysa[rows, h // 2, t0:t0 + n], mix[half][rows, 768:768 + n], ACT.Copy).then_inc(at_out, 1)

                nc.scalar.drain()
                act.wait_ge(at_out, l * 40 + 40)
                act.dma_start(y_dram, y_mix[:, :, :]).then_inc(y_away, 16)
                act.wait_ge(out_stored, l * OUTS + 80)
                act.dma_start(lora_wa, layer_of(dr["lora_wa"], l)).then_inc(in_rw, 16)
                act.dma_start(lora_g, layer_of(dr["lora_g"], l)).then_inc(in_g2, 16)
                act.dma_start(cmask, dr["cmask"]).then_inc(in_rw, 16)
                act.dma_start(Z1, layer_of(dr["st_rw"], l)).then_inc(in_rw, 16)
                act.wait_ge(shift_dve, l * N_RW + N_RW)
                act.dma_start(layer_of(outs["shift"], l), shift_out).then_inc(out_stored, 16)
                def kk_squares(tiles):
                    for j in tiles:
                        act.wait_ge(lora_dve.sem, lora_dve.at(f"kk0_{j}", l))
                        if j >= 2:
                            act.wait_ge(lora_pe.sem, lora_pe.at(f"ssq{j - 2}", l))
                        op(sq_t[:, j % 2, :], a_kk[:, j, :], ACT.Square).then_inc(lora_act.sem, 1)

                kk_squares(range(0, 2))
                op(xwa[0:C, :], xwa[0:C, :], ACT.Tanh)
                op(xg, xg, ACT.Sigmoid)
                kk_squares(range(2, 4))
                act.wait_ge(lw_clear, l + 1)
                for j in range(4):
                    w_ps, a_ps = (mix, dense)[j % 2]
                    act.wait_ge(lora_pe.sem, lora_pe.at(f"lora{j}", l))
                    if j >= 2:
                        act.wait_ge(lora_dve.sem, lora_dve.at(f"scan{j - 2}", l))
                    lwv = lw[:, j % 2, :].rearrange("p (c t) -> p c t", t=65)[:, :, 1:65]
                    op(lwv[:, 0:8, :], w_ps[:, 0:TP].rearrange("p (c t) -> p c t", t=C), ACT.Sigmoid, bias=pr("w0", j))
                    op(lwv[:, 8, :], w_ps[:, SX:TX], ACT.Sigmoid, bias=pr("w0", j))
                    op(a_b[:, j, :], a_ps[:, 0:TX], ACT.Sigmoid, bias=pr("a0", j)).then_inc(lora_act.sem, 1)
                nc.scalar.preload_act_table_set(EXP_LN)
                act.wait_ge(lora_dve.sem, lora_dve.at("clamp3", l))
                op(clamped[:, :, :], clamped[:, :, :], ACT.Ln, scale=2.0 ** 24)
                nc.scalar.drain()
                for j in range(4):
                    op(clamped[:, j, :], clamped[:, j, :], ACT.Exp, scale=-0.5, bias=small[:, 2:3]).then_inc(lora_act.sem, 1)
                act.wait_ge(lora_dve.sem, lora_dve.at("kk3", l))
                act.wait_ge(out_stored, l * OUTS + 96)
                rwkv_stage(l, 0)
                for body, (f, s) in enumerate(RW_BODIES):
                    rwkv_body(l, body, f, s)
                    if s == R5 - 2:
                        act.wait_ge(ch_z, l * C9 + (START + 8))
                        act.dma_start(layer_of(outs["st_rw_p"], l), Z0).then_inc(out_stored, 16)
                        act.dma_start(x[:, :, :], x_dram).then_inc(x_back, 16)
                act.wait_ge(ch_z, l * C9 + (START + 9))
                act.dma_start(layer_of(outs["st_rw_s"], l), Z1).then_inc(out_stored, 16)
                act.dma_start(y_mix[:, :, :], y_dram).then_inc(y_back, 16)
                for p in range(2):
                    act.wait_ge(gate_stored[p], l * (16 * N_GATE // 2) + 16 * N_GATE // 2)
                for g in range(2):
                    for p in (0, 1):
                        act.wait_ge(gn_dve.sem, gn_dve.at(f"yc{p}", l, g))
                        op(p_sq[:, p, :], p_y[:, p, :], ACT.Square).then_inc(gn_act.sem, 1)
                    for p in (0, 1):
                        act.wait_ge(gn_pe.sem, gn_pe.at(f"var{p}", l, g))
                        root(p_rs[:, p, :], (mix, dense)[p][1], TX, 1.0 / C, 1).then_inc(gn_act.sem, 1)
                act.wait_ge(br_split, l * 12 + 8)
                def load_gate(n):
                    mp, b, mi = n // 6, n // 2 % 3, n % 2
                    if n >= 3:
                        u = U_BR + n - 3
                        act.wait_ge(dense_free[u % 2], free_before(u, l, 1))
                    act.dma_start(gate_in[:, n % 3, :], gate_dram[b * KT + mp * 2 + mi]).then_inc(in_gate[n % 3], 16)

                for n in range(2):
                    load_gate(n)
                for n in range(24):
                    if n + 2 < 24:
                        load_gate(n + 2)
                    act.wait_ge(in_gate[n % 3], l * 128 + (16 * (n // 3) + 16))
                    op(gate_in[:, n % 3, :], gate_in[:, n % 3, :], ACT.Sigmoid).then_inc(gate_ready, 1)
                squares(l * 2 + 1, after_dve(l, U_WO))
                norm_root(l * 2 + 1)
                high_parts(l, 1)
                with act.Fori(0, FF) as c:
                    for m in range(KT):
                        act.wait_ge(w_used, used_after(T_MLP + m, l) + c * (4 * KT))
                        if m >= 2:
                            act.wait_ge(mlp_split, START + l * (FF * KT) + c * KT + m - 1)
                        else:
                            act.wait_ge(mlp_split, START + l * (FF * KT) + c * KT)
                        op(halves(relu_m[:, m % 2, :]), out_of(dense[m % 2]), ACT.Relu).then_inc(dense_free[m % 2], 1)
                        nc.scalar.drain()
                        op(sq_m[:, m % 2, :], relu_m[:, m % 2, :], ACT.Square).then_inc(mlp_act, 1)
                squares(l * 2 + 2, after_dve(l, U_MLP + (FF - 1) * 2 * KT + KT))
            norm_root(2 * DEPTH)
            act.wait_ge(fin, KT)
            act.dma_start(outs["y"], x[:, :, :]).then_inc(out_stored, 16)
            act.wait_ge(out_stored, DEPTH * OUTS + 16)

        @block.vector
        def _(dve):
            v = nc.vector

            def settle():
                v.drain()

            def passed():
                dve.sem_inc(waited_dve, 1)

            def norm_apply(n, l, which, gain):
                dve.wait_ge(rs_ready, n + 1)

                def low(k):
                    dve.wait_ge(high_ready, l * (2 * KT) + (which * KT + k + 1))
                    v.tensor_tensor(act_lo[:, k, :], n_t[:, k % 2, :], act_hi[:, k, :].bitcast(F32),
                                    ALU.subtract).then_inc(act_ready, 1)
                    settle()

                for k in range(KT):
                    if k >= 2:
                        low(k - 2)
                    v.scalar_tensor_tensor(n_t[:, k % 2, :], x[:, k, :], gain(k), n_rs, ALU.mult,
                                           ALU.mult).then_inc(normed, 1)
                low(KT - 2)
                low(KT - 1)

            def rope(l, n, raw, tc, tr, cos, sin, dst, rows=P):
                s = slice(0, rows)
                dve.wait_ge(rope_raw, l * 16 + (n + 1))
                v.tensor_tensor(tc[s, n % 2, :], raw[s, n % 2, :], cos[s], ALU.mult)
                dve.wait_ge(rope_rot, l * 16 + (n + 1))
                v.tensor_tensor(tr[s, n % 2, :], mix[n % 2][s, 0:T], sin[s], ALU.mult)
                settle()
                v.tensor_tensor(dst, tc[s, n % 2, :], tr[s, n % 2, :], ALU.add).then_inc(rope_done, 1)

            def retention_step(l, i, n, s_in, s_mid, s_out):
                ch = l * C9 + 2 * i
                tok = bass.ds(i * P, n)
                dve.wait_ge(ret_cross, START + ch)
                v.tensor_copy(k_st[:, :, 0:n], rk[:, :, tok])
                v.tensor_copy(v_st[:, :, 0:n], rv[:, :, tok])
                v.tensor_copy(q_st[:, :, 0:n], rq[:, :, tok])
                v.tensor_tensor(q_dec[:, :, 0:n], rq[:, :, tok], r_qdec[:, :, 0:n], ALU.mult).then_inc(ret_dve.sem, 1)
                dve.wait_ge(ret_pe.sem, ret_pe.at("turned", l, i))
                v.tensor_tensor(k_tm[0:n], bank[0][0:n, :].rearrange("p (h e) -> p h e", e=P),
                                r_kdec[0:n].unsqueeze(2).broadcast_to([n, 4, P]), ALU.mult).then_inc(ret_dve.sem, 1)
                dve.wait_ge(ret_pe.sem, ret_pe.at("gram", l, i))
                v.tensor_tensor(sc_sb[0:n, :, 0:n], bank[2][0:n, :].rearrange("p (h t) -> p h t", t=P)[:, :, 0:n],
                                r_dmask[0:n, :, 0:n], ALU.mult).then_inc(ret_dve.sem, 1)
                for q, (a, z) in enumerate([(s_in, s_mid), (s_mid, s_out)][0:n // C]):
                    v.tensor_tensor(st_t[:, :, :], a[:, :, :], r_gam[:, :, :], ALU.mult)
                    settle()
                    if q:
                        dve.wait_ge(ret_cross, START + ch + 1)
                    else:
                        dve.wait_ge(ret_pe.sem, ret_pe.at("state", l, i))
                    v.tensor_tensor(z[:, :, :], st_t[:, :, :], bank[q].rearrange("p (h e) -> p h e", e=P),
                                    ALU.add).then_inc(ret_state, 1)
                    settle()

            def rwkv_stage(l, f):
                nq, (al, rh, _, _, TkT, *_) = STEP_CHUNKS[f], sets[f % 2]
                t0 = f * P if f < R5 - 1 else SX
                tok = slice(t0, t0 + nq * C)
                view = lambda t: t[:, 0:4 * nq * C].rearrange("p (j t) -> p j t", j=4)
                dve.wait_ge(rw_exp, l * R5 + (f + 1))
                v.tensor_copy(w_ends[f % 2][:, 0:4 * nq], blocks3(rh, 4 * nq)[:, :, C - 1])
                v.tensor_tensor(view(be), a_b[:, :, tok], view(ka), ALU.mult)
                v.tensor_tensor(view(al), a_kk[:, :, tok], view(al), ALU.mult)
                settle()
                v.tensor_tensor(view(ka), a_k[:, :, tok], view(ka), ALU.mult)
                v.tensor_tensor(view(rh), a_r[:, :, tok], view(rh), ALU.mult)
                v.tensor_copy(view(TkT), a_v[:, :, tok]).then_inc(rw_staged, 1)

            def rwkv_body(l, body, f, s):
                if f is not None:
                    g, w = 4 * STEP_CHUNKS[f], 4 * STEP_CHUNKS[f] * C
                    al, rh, LkT, TbT, TkT, Vt, kat, bet, XT = sets[f % 2]

                    def gram():
                        dve.wait_ge(rw_pe.sem, rw_pe.at("gram", l, f))
                        v.tensor_tensor(blocks3(XX, g), blocks3(bank[1], g), mask3(M_PAIR_T, g), ALU.mult)
                        v.tensor_tensor(blocks3(LkT, g), blocks3(bank[2], g), mask3(M_STRICT, g), ALU.mult)
                        v.tensor_tensor(blocks3(TbT, g), blocks3(bank[3], g), mask3(M_INCL, g), ALU.mult).then_inc(rw_dve.sem, 1)
                        dve.wait_ge(rw_act.sem, rw_act.at("lt", l, f))
                        v.tensor_tensor(blocks3(XT, g), blocks3(LT, g), mask3(M_PAIR, g), ALU.mult)
                        settle()
                        v.tensor_tensor(blocks3(BTs[0], g), blocks3(LT, g), mask3(M_LEVEL, g), ALU.mult)
                        v.tensor_tensor(blocks3(XX, g), mask3(M_EYE, g), blocks3(XX, g), ALU.subtract)
                        v.tensor_tensor(blocks3(XT, g), mask3(M_EYE, g), blocks3(XT, g), ALU.subtract).then_inc(rw_dve.sem, 1)

                    def turn():
                        dve.wait_ge(rw_pe.sem, rw_pe.at("turned", l, f))
                        v.tensor_tensor(blocks3(TkT, g), blocks3(bank[0], g), mask3(M_INCL, g), ALU.mult).then_inc(rw_dve.sem, 1)
                        settle()

                    def level(n):
                        if n < last:
                            v.tensor_tensor(blocks3(BTs[(n + 1) % 2], g), blocks3(LT, g), mask3(M_LEVEL + n + 1, g), ALU.mult)
                        for h in (0, 1):
                            b = slice(h * w // 2, (h + 1) * w // 2)
                            dve.wait_ge(rw_pe.sem, rw_pe.at(f"x_{n}_{h}", l, f))
                            if n < last:
                                v.tensor_tensor(XX[:, b], XX[:, b], bank[1 + h][:, 0:w // 2], ALU.subtract).then_inc(rw_dve.sem, 1)
                            v.tensor_tensor(XT[:, b], XT[:, b], bank[1 + h][:, 256:256 + w // 2], ALU.subtract).then_inc(rw_dve.sem, 1)
                        settle()
                        if n == last - 1 and f + 1 < R5:
                            rwkv_stage(l, f + 1)

                if s is not None:
                    nq = STEP_CHUNKS[s]
                    Z = (Z0, Z1)[s == R5 - 1]

                    def chunk_z(q):
                        dve.wait_ge(ch_pe.sem, ch_pe.at("z", l, 2 * s + q))
                        v.tensor_tensor(z_t, Z, z_ps, ALU.add)
                        settle()
                        dve.wait_ge(ch_pe.sem, ch_pe.at("y", l, 2 * s + q))
                        decay = w_ends[s % 2][:, 0:4 * nq].rearrange("p (j q) -> p j q", q=nq)[:, :, q]
                        v.tensor_tensor(blocks3(Z, 4), blocks3(z_t, 4), decay.unsqueeze(2).broadcast_to([P, 4, C]),
                                        ALU.mult).then_inc(ch_z, 1)
                        settle()

                if s is None:
                    gram()
                    turn()
                    for n in range(last + 1):
                        level(n)
                elif f is None:
                    for q in range(nq):
                        chunk_z(q)
                else:
                    gram()
                    turn()
                    chunk_z(0)
                    level(0)
                    level(1)
                    chunk_z(1)
                    for n in range(2, last + 1):
                        level(n)

            dve.wait_ge(in_x, 16)
            dve.wait_ge(in_const, 48)
            with dve.Fori(0, DEPTH) as l:
                dve.wait_ge(in_par, l * 16 + 16)
                norm_apply(l * 2, l, 0, lambda k: pr("g1", k))
                dve.wait_ge(in_ret, l * 48 + 48)
                for n in range(8):
                    rope(l, n, t_raw, t_cos, t_rot, r_cos, r_sin, rq[:, n, :] if n < 4 else rk[:, n - 4, :])
                v.memset(st0[:, :, :], 0.0)
                for h in range(4):
                    u = 12 + h
                    dve.wait_ge(ret_sig, l * 4 + (h + 1))
                    v.tensor_tensor(halves(rg[:, h, :]), out_of(dense[u % 2]), halves(rg[:, h, :]), ALU.mult).then_inc(dense_free[u % 2], 1)
                settle()
                with dve.Fori(0, 4) as i:
                    retention_step(l, i, P, st0, st1, st0)
                retention_step(l, 4, C, st_s, st1, None)
                for h in range(4):
                    dve.wait_ge(post_act.sem, post_act.at(f"rs{h}", l))
                    v.tensor_tensor(t_rot[:, h % 2, :], yret[:, h, :], t_cos[:, h % 2, :], ALU.mult)
                    settle()
                    v.tensor_tensor(yret[:, h, :], t_rot[:, h % 2, :], rg[:, h, :], ALU.mult).then_inc(post_dve, 1)

                dve.wait_ge(out_stored, l * OUTS + 32)
                dve.wait_ge(in_sa, l * 128 + 128)
                for n in range(8, 16):
                    rows = C if n == 15 else P
                    dst = ysa[:, n - 8, :] if n < 12 else k_rope if n == 12 else qi[:, n - 13, :] if n < 15 else ki[0:C, 0:T]
                    rope(l, n, s_raw, s_tcos, s_trot, s_cos, s_sin, dst, rows)
                settle()
                for kv in range(2):
                    for half in range(2):
                        v.tensor_copy(kd[half * C:half * C + C, kv, 0:T], k_rope[kv * C:kv * C + C])
                v.tensor_copy(ki[C:P, 0:T], ki[0:C, 0:T])
                dve.wait_ge(sa_pe, l + 1)
                v.tensor_copy(wi[:, 0:4, :], bank[2].rearrange("p (b e) -> p b e", e=P)[:, :, C:C + 4])
                v.tensor_copy(wi[0:C, 4, :], bank[3][0:C, C:C + 4]).then_inc(sa_dve, 1)
                settle()
                v.memset(pt[:, :, 0:1], 0.0)
                settle()
                shifted = [a[:, j, :] for a in (a_r, a_k, a_v) for j in range(4)] + [xwa, xg]

                def token_shift(tiles):
                    for t in tiles:
                        if t >= N_RW:
                            continue
                        cur = pt[:, t % 2, :]
                        dve.wait_ge(shift_act, l * N_RW + (t + 1))
                        v.tensor_tensor(d_t, cur[:, 0:TX], cur[:, 1:TX + 1], ALU.subtract)
                        v.tensor_copy(shift_out[:, t:t + 15:14], cur[:, TP:TX + 1:65])
                        settle()
                        v.scalar_tensor_tensor(shifted[t], d_t, pr("mu", t), cur[:, 1:TX + 1], ALU.mult,
                                               ALU.add).then_inc(shift_dve, 1)
                        settle()

                for b in range(5):
                    n = P if b < 4 else C
                    keys = (b + 1) * P if b < 4 else T
                    if b == 0:
                        v.memset(bias[:, 0:P], 0.0)
                        settle()
                        v.memset(bias[0:C, C:P], NEG)
                        settle()
                    else:
                        for i in range(4):
                            dve.wait_ge(ix_act, l * 16 + (b - 1) * 4 + i + 1)
                            rel, hw = relu_sb[0:n, i % 2, 0:keys], wi[0:n, b, i:i + 1]
                            sc = score[0:n, 0:keys]
                            if i == 0:
                                v.tensor_scalar(sc, rel, hw, None, ALU.mult).then_inc(ix_dve, 1)
                            else:
                                v.scalar_tensor_tensor(sc, rel, hw, sc, ALU.mult, ALU.add).then_inc(ix_dve, 1)
                            settle()
                        if b < 4:
                            v.memset(score[0:C, keys - C:keys], FILL)
                            settle()
                        rounds = (TOPK_P if b < 4 else TOPK_S) // 8
                        with dve.Fori(0, rounds // 2):
                            for _ in range(2):
                                v.max(out=top8[0:n], in_=sc)
                                settle()
                                v.match_replace(out=sc, in_to_replace=top8[0:n], in_values=sc, imm_value=MARK)
                                settle()
                        v.tensor_scalar(bias[0:n, 0:keys], sc, EDGE, NEG, ALU.is_gt, ALU.mult)
                        settle()

                    def logits(h):
                        half, run = h % 2, b * 8 + h
                        dve.wait_ge(at_scores, l * 40 + (run + 1))
                        if h >= 2:
                            dve.wait_ge(at_exp, l * 40 + (run - 1))
                        passed()
                        v.tensor_tensor_reduce(logit[0:n, half, 0:keys], mix[half][0:n, 0:keys], bias[0:n, 0:keys],
                                               SA_SCALE, -3.0e38, ALU.add, ALU.max, stat[0:n, half, 0:1])
                        settle()
                        v.tensor_scalar(stat[0:n, half, 1:2], stat[0:n, half, 0:1], -1.0, None,
                                        ALU.mult).then_inc(at_logits, 1)

                    token_shift(done(*fill_range(b)))
                    logits(0)
                    for h in range(8):
                        half, run = h % 2, b * 8 + h
                        dve.wait_ge(at_exp, l * 40 + (run + 1))
                        v.reciprocal(stat[0:n, half, 3:4], stat[0:n, half, 2:3])
                        settle()
                        v.tensor_scalar(prob[0:n, half, 0:keys], prob[0:n, half, 0:keys], stat[0:n, half, 3:4], None,
                                        ALU.mult).then_inc(at_probs, 1)
                        if h < 7:
                            logits(h + 1)
                        token_shift(done(*fill_range(b, h, 0)))
                        token_shift(done(*fill_range(b, h, 1)))

                dve.wait_ge(at_out, l * 40 + 40)
                dve.wait_ge(out_stored, l * OUTS + 80)
                for p in range(2):
                    dve.wait_ge(gate_stored[p], l * (16 * N_GATE // 2) + 16 * GATES_DSA // 2)
                for j in range(4):
                    v.tensor_scalar(a_kk[:, j, :], a_k[:, j, :], pr("k_k", j), None, ALU.mult).then_inc(lora_dve.sem, 1)
                v.memset(Z0, 0.0)
                v.memset(lw[:, :, :], 0.0).then_inc(lw_clear, 1)
                settle()
                for j in range(4):
                    dve.wait_ge(lora_pe.sem, lora_pe.at(f"ssq{j}", l))
                    v.tensor_scalar(clamped[:, j, :], dense[j % 2][:, 0:TX], 1e-24, None, ALU.max).then_inc(lora_dve.sem, 1)
                dve.wait_ge(in_rw, l * 48 + 48)
                for j in range(4):
                    dve.wait_ge(lora_act.sem, lora_act.at(f"sig{j}", l))
                    v.tensor_tensor_scan(cum[:, j, :], cmask, lw[:, j % 2, :], 0.0, ALU.mult, ALU.add).then_inc(lora_dve.sem, 1)
                    v.tensor_scalar(d_t, a_b[:, j, :], -1.0, pr("k_a", j), ALU.add, ALU.mult)
                    settle()
                    v.scalar_tensor_tensor(a_k[:, j, :], d_t, 1.0, a_k[:, j, :], ALU.add, ALU.mult)
                    settle()
                for j in range(4):
                    dve.wait_ge(lora_act.sem, lora_act.at(f"norm{j}", l))
                    v.tensor_tensor(a_kk[:, j, :], a_kk[:, j, :], clamped[:, j, :], ALU.mult)
                    settle()
                    v.tensor_tensor(a_b[:, j, :], a_kk[:, j, :], a_b[:, j, :], ALU.mult).then_inc(lora_dve.sem, 1)
                settle()
                dve.wait_ge(out_stored, l * OUTS + 96)
                passed()
                rwkv_stage(l, 0)
                for body, (f, s) in enumerate(RW_BODIES):
                    rwkv_body(l, body, f, s)
                dve.wait_ge(out_stored, l * OUTS + OUTS)
                for p in range(2):
                    dve.wait_ge(gate_stored[p], l * (16 * N_GATE // 2) + 16 * N_GATE // 2)
                for g in range(2):
                    tiles = [(p, 2 * g + p, (mix, dense)[p]) for p in (0, 1)]
                    for p, j, ps in tiles:
                        dve.wait_ge(gn_pe.sem, gn_pe.at(f"mean{p}", l, g))
                        v.scalar_tensor_tensor(p_y[:, p, :], ps[0][:, 0:TX], -1.0 / C, a_kk[:, j, :], ALU.mult,
                                               ALU.add).then_inc(gn_dve.sem, 1)
                    for p, j, ps in tiles:
                        v.scalar_tensor_tensor(p_rk[:, p, :], a_r[:, j, :], pr("r_k", j), a_k[:, j, :], ALU.mult,
                                               ALU.mult).then_inc(gn_dve.sem, 1)
                    for p, j, ps in tiles:
                        dve.wait_ge(gn_pe.sem, gn_pe.at(f"bonus{p}", l, g))
                        v.tensor_tensor(p_bv[:, p, :], ps[0][:, 0:TX], a_v[:, j, :], ALU.mult)
                        dve.wait_ge(gn_act.sem, gn_act.at(f"rs{p}", l, g))
                        v.scalar_tensor_tensor(p_y[:, p, :], p_y[:, p, :], pr("lnx", j), p_rs[:, p, :], ALU.mult, ALU.mult)
                    settle()
                    v.tensor_tensor(p_y[:, :, :], p_y[:, :, :], p_bv[:, :, :], ALU.add)
                    settle()
                    for p, j, ps in tiles:
                        dve.wait_ge(gn_pe.sem, gn_pe.at(f"gate{p}", l, g))
                        v.tensor_tensor(a_kk[:, j, :], ps[1][:, 0:TX], p_y[:, p, :], ALU.mult).then_inc(gn_dve.sem, 1)
                    settle()
                for b in range(3):
                    if b:
                        dve.wait_ge(y_back, l * 16 + 16)
                    for k in range(4):
                        if b == 0:
                            v.tensor_copy(in_hi[:, k, 0:TP], a_kk[:, k, 0:TP])
                            v.tensor_copy(in_hi[:, k, TP:T], a_kk[:, k, SX:TX])
                        else:
                            v.tensor_copy(in_hi[:, b * 4 + k, :], (ysa, yret)[b - 1][:, k, :])
                    settle()
                    for k in range(4):
                        hi = in_hi[:, b * 4 + k, :].bitcast(F32)
                        lo = in_lo[:, b * 4 + k, :]
                        if b == 0:
                            v.tensor_tensor(lo[:, 0:TP], a_kk[:, k, 0:TP], hi[:, 0:TP], ALU.subtract)
                            v.tensor_tensor(lo[:, TP:T], a_kk[:, k, SX:TX], hi[:, TP:T], ALU.subtract).then_inc(br_split, 1)
                        else:
                            v.tensor_tensor(lo, (ysa, yret)[b - 1][:, k, :], hi, ALU.subtract).then_inc(br_split, 1)
                settle()
                for n in range(24):
                    mp, b, mi = n // 6, n // 2 % 3, n % 2
                    u = U_BR + n
                    dve.wait_ge(w_used, used_after(T_BR + n // 2, l, 0 if mi else 1))
                    dve.wait_ge(gate_ready, l * 24 + (n + 1))
                    ps, gate = out_of(dense[u % 2]), halves(gate_in[:, n % 3, :])
                    if b == 0:
                        v.tensor_tensor(halves(merged[:, mi, :]), ps, gate, ALU.mult).then_inc(dense_free[u % 2], 1)
                        continue
                    v.tensor_tensor(halves(gated[:, mi, :]), ps, gate, ALU.mult).then_inc(dense_free[u % 2], 1)
                    settle()
                    v.tensor_tensor(merged[:, mi, :], merged[:, mi, :], gated[:, mi, :], ALU.add)
                    settle()
                    if b == 2:
                        m = mp * 2 + mi
                        v.tensor_copy(act_hi[:, m, :], merged[:, mi, :])
                        settle()
                        v.tensor_tensor(act_lo[:, m, :], merged[:, mi, :], act_hi[:, m, :].bitcast(F32),
                                        ALU.subtract).then_inc(br_gated, 1)
                        settle()
                dve.wait_ge(x_back, l * 16 + 16)
                for m in range(KT):
                    u = U_WO + m
                    dve.wait_ge(w_used, used_after(T_WO + m, l))
                    v.tensor_tensor(halves(x[:, m, :]), halves(x[:, m, :]), out_of(dense[u % 2]), ALU.add).then_inc(dense_free[u % 2], 1)
                settle()
                norm_apply(l * 2 + 1, l, 1, lambda k: pr("g2", k))
                settle()
                with dve.Fori(0, FF) as c:
                    for m in range(KT):
                        dve.wait_ge(mlp_act, l * (FF * KT) + c * KT + m + 1)
                        v.tensor_copy(in_hi[:, m, :], sq_m[:, m % 2, :])
                        settle()
                        v.tensor_tensor(in_lo[:, m, :], sq_m[:, m % 2, :], in_hi[:, m, :].bitcast(F32),
                                        ALU.subtract).then_inc(mlp_split, 1)
                    for m in range(KT):
                        dve.wait_ge(w_used, used_after(T_MLP + KT + m, l) + c * (4 * KT))
                        v.tensor_tensor(halves(x[:, m, :]), halves(x[:, m, :]), out_of(dense[m % 2]), ALU.add).then_inc(dense_free[m % 2], 1)
                    settle()
            dve.wait_ge(rs_ready, 2 * DEPTH + 1)
            for k in range(KT):
                v.scalar_tensor_tensor(x[:, k, :], x[:, k, :], small[:, 8 + k:9 + k], n_rs, ALU.mult, ALU.mult).then_inc(fin, 1)



def channel_tiles(a):
    return np.moveaxis(a.reshape(a.shape[:-1] + (-1, P)), -1, -2)


def rope_tables(width, freqs, rows):
    pos = np.concatenate([np.arange(TP), TP + np.arange(TS)]).astype(np.float32)
    ang = (pos[:, None] * freqs[None, :].astype(np.float32)).astype(np.float32)
    half = len(freqs)
    cos, sin = np.ones((rows, T), np.float32), np.zeros((rows, T), np.float32)
    for h in range(0, rows, width):
        for part in (0, half):
            cos[h + part:h + part + half] = np.cos(ang).T
            sin[h + part:h + part + half] = np.sin(ang).T
    return np.concatenate([cos, sin], 1)


def rotation(width, half):
    r = np.zeros((P, P), np.float32)
    for h in range(0, P, width):
        for i in range(half):
            r[h + half + i, h + i] = -1.0
            r[h + i, h + half + i] = 1.0
    return r


def constants():
    f32 = np.float32
    eye = np.eye(P, dtype=f32)
    blk = np.kron(np.eye(2, dtype=f32), np.ones((C, C), f32))
    cst = np.concatenate([eye, np.ones((P, P), f32), blk, rotation(64, 8), rotation(128, 64)], 1)
    s, t = np.meshgrid(np.arange(C), np.arange(C), indexing="ij")
    level = lambda h: (s // (2 * h) == t // (2 * h)) & (s % (2 * h) < h) & (t % (2 * h) >= h)
    m = [s < t, s <= t, level(1), level(1).T, s == t] + [level(h) for h in LEVELS]
    masks = np.stack([np.concatenate([a, a], 0) for a in m], 1).astype(f32)
    small = np.zeros((P, 16), f32)
    small[:, 0], small[:, 1], small[:, 2] = EPS, GN_EPS, 12 * np.log(2.0)
    lg = np.log1p(-np.exp2(-5.0 - np.arange(4)))
    i = np.arange(P)
    same = (i[:, None] // C) == (i[None, :] // C)
    dmask = np.exp(np.abs(i[:, None] - i[None, :])[:, None, :] * lg[None, :, None]) * same[:, None, :]
    gam = np.broadcast_to(np.exp(C * lg)[None, :, None], (P, 4, P))
    qdec = np.broadcast_to(np.exp((i % C + 1)[None, None, :] * lg[None, :, None]), (P, 4, P))
    kdec = np.exp((C - 1 - i % C)[:, None] * lg[None, :])
    r_con = np.concatenate([dmask.reshape(P, -1), gam.reshape(P, -1), qdec.reshape(P, -1), kdec], 1).astype(f32)
    sa_f = (1.0 / (500000.0 ** (np.arange(0, 16, 2, dtype=f32) / 16))).astype(f32)
    ret_f = (1.0 / (10000.0 ** np.linspace(0.0, 1.0, 64, dtype=f32))).astype(f32)
    cmask = np.ones((P, NC, 65), f32)
    cmask[:, :, 0] = 0.0
    return {"cst": cst, "masks": masks, "small": small, "r_con": r_con, "cmask": cmask.reshape(P, -1),
            "r_tab": rope_tables(128, ret_f, P), "s_tab": rope_tables(64, sa_f, P)}


def weight_tiles(w):
    n = w.shape[1] // P
    return w.reshape(KT, P, n, P).transpose(2, 1, 0, 3).reshape(n, P, KT * P)


def kernel(**inputs):
    import concourse.bacc as bacc
    from concourse.bass_utils import run_bass_kernel_spmd

    a = {k: np.asarray(v) for k, v in inputs.items()}
    arrays = constants()
    arrays["x"] = np.ascontiguousarray(
        np.concatenate([a["x_prompt"][0], a["x_sample"][0]], 0).reshape(T, KT, P).transpose(2, 1, 0))
    arrays["small"] = np.concatenate([arrays["small"][:, 0:8], channel_tiles(a["final_norm_g"])], 1)
    stream = []
    for l in range(DEPTH):
        w = a["w_in"][l]
        rw, sa, ret, gate = np.split(w, [1792, 2884, 4932], 1)
        pad = lambda m, n: np.concatenate([m, np.zeros((m.shape[0], n), m.dtype)], 1)
        stream += [weight_tiles(ret), weight_tiles(pad(sa, 60)), weight_tiles(rw), weight_tiles(pad(gate, P))]
        br = np.stack([a[n][l] for n in ("w_br_rwkv", "w_br_dsa", "w_br_ret")])
        stream.append(br.reshape(3, 4, P, 4, 2, P).transpose(3, 0, 2, 4, 1, 5).reshape(12, P, 8 * P))
        stream.append(weight_tiles(a["w_o"][l]))
        for c in range(FF):
            stream.append(weight_tiles(a["w_up"][l][:, c * D:(c + 1) * D]))
            stream.append(weight_tiles(a["w_down"][l][c * D:(c + 1) * D, :]))
    arrays["stream"] = np.ascontiguousarray(np.concatenate(stream, 0))
    cols = {"g1": a["norm1_g"], "g2": a["norm2_g"], "mu": a["rwkv_mu"], "w0": a["rwkv_w0"], "a0": a["rwkv_a0"],
            "k_k": a["rwkv_k_k"], "k_a": a["rwkv_k_a"], "r_k": a["rwkv_r_k"].reshape(DEPTH, -1),
            "lnx": a["rwkv_lnx_g"], "shift": a["state_rwkv_shift"][:, 0]}
    arrays["par"] = np.concatenate([channel_tiles(cols[n]) for n in PARAMS], 2)
    arrays["lora_wa"] = np.concatenate([a["rwkv_w2"], a["rwkv_a2"]], 1)
    arrays["lora_g"] = a["rwkv_g2"]
    arrays["st_ret"] = a["state_ret"][:, 0].transpose(0, 2, 1, 3).reshape(DEPTH, P, 512)
    arrays["st_rw"] = a["state_rwkv"][:, 0].reshape(DEPTH, 4, 2, C, C).transpose(0, 2, 4, 1, 3).reshape(DEPTH, P, 256)
    arrays["k_old"] = a["cache_dsa_k"][:, 0].reshape(DEPTH, TP, P).transpose(0, 2, 1)
    arrays["ik_old"] = a["cache_dsa_ik"][:, 0].transpose(0, 2, 1)
    arrays["v_old"] = a["cache_dsa_v"][:, 0].reshape(DEPTH, 4, P, P).transpose(0, 2, 1, 3).reshape(DEPTH, P, 512)
    arrays = {k: np.ascontiguousarray(v) for k, v in arrays.items()}

    nc = bacc.Bacc("TRN2", target_bir_lowering=False, num_devices=1)
    dr = {k: nc.dram_tensor(f"in_{k}", v.shape, mybir.dt.from_np(v.dtype), kind="ExternalInput").ap()
          for k, v in arrays.items()}
    shapes = {"y": (P, KT, T), "k_new": (DEPTH, P, T), "v_new": (DEPTH, P, T), "ik_new": (DEPTH, C, T),
              "shift": (DEPTH, P, 28), "st_rw_p": (DEPTH, P, 256), "st_rw_s": (DEPTH, P, 256),
              "st_ret_p": (DEPTH, P, 512), "st_ret_s": (DEPTH, P, 512)}
    outs = {k: nc.dram_tensor(f"out_{k}", s, F32, kind="ExternalOutput").ap() for k, s in shapes.items()}
    build(nc, dr, outs)
    r = run_bass_kernel_spmd(nc, [{f"in_{k}": v for k, v in arrays.items()}], core_ids=[0]).results[0]
    o = {k: r[f"out_{k}"] for k in shapes}

    y = o["y"].transpose(2, 1, 0).reshape(T, D)
    kv = lambda n, s: o[n][:, :, s].transpose(0, 2, 1).reshape(DEPTH, 1, -1, 2, C)
    ik = lambda s: o["ik_new"][:, :, s].transpose(0, 2, 1)[:, None]
    rw = lambda n: o[n].reshape(DEPTH, 2, C, 4, C).transpose(0, 3, 1, 4, 2).reshape(DEPTH, 1, 8, C, C)
    ret = lambda n: o[n].reshape(DEPTH, P, 4, P).transpose(0, 2, 1, 3)[:, None]
    shift = lambda i: o["shift"][:, :, 14 * i:14 * i + 14].transpose(0, 2, 1).reshape(DEPTH, 1, 1792)
    pr, sa = slice(0, TP), slice(TP, T)
    return (y[None, :TP], y[None, TP:],
            kv("k_new", pr), kv("v_new", pr), ik(pr), rw("st_rw_p"), shift(0), ret("st_ret_p"),
            kv("k_new", sa), kv("v_new", sa), ik(sa), rw("st_rw_s"), shift(1), ret("st_ret_s"))
```
